# Optimizing a Trainium2 kernel written in Bass

```python
import jax, jax.numpy as jnp
from jax import lax
import numpy as np

D_MODEL = 1024
BATCH = 1
SEQ = 2048
DEPTH = 2

HEAD_DIM = 64
BLK = 128
ROPE_THETA = 500000.0
ROT_DIM = HEAD_DIM // 4
EPS = 1e-6
SGU_GROUPS = 8
SGU_WIDTH = SGU_GROUPS * HEAD_DIM
SGU_CHUNK = 128
DIL_GROUPS = ((128, 1), (512, 4), (2048, 16))
DIL_HPG = 4
DIL_HEADS = DIL_HPG * len(DIL_GROUPS)
DIL_WIDTH = DIL_HEADS * HEAD_DIM
SWA_Q_HEADS = 16
SWA_KV_HEADS = 2
SWA_WINDOW = 128
N_GROUPS = 4
EXPERTS_PER_GROUP = 8
N_EXPERTS = N_GROUPS * EXPERTS_PER_GROUP
EXPERT_FF = 256
TOP_K = 2
MOE_BLOCK = 128
N_EVEN = (DEPTH + 1) // 2
N_ODD = DEPTH // 2
IN_EVEN = 2 * SGU_WIDTH + 3 * DIL_WIDTH
OUT_EVEN = SGU_WIDTH + DIL_HPG * HEAD_DIM
EVEN_SPLITS = (SGU_WIDTH, 2 * SGU_WIDTH, 2 * SGU_WIDTH + DIL_WIDTH, 2 * SGU_WIDTH + 2 * DIL_WIDTH)
IN_ODD = (SWA_Q_HEADS + 2 * SWA_KV_HEADS) * HEAD_DIM
OUT_ODD = SWA_Q_HEADS * HEAD_DIM
ODD_SPLITS = (SWA_Q_HEADS * HEAD_DIM, (SWA_Q_HEADS + SWA_KV_HEADS) * HEAD_DIM)

kernel_name = "hybrid_sgu_dilated_swa_sink_hmoe"

def rms_norm(x, g):
    xf = x.astype(jnp.float32)
    y = xf * lax.rsqrt(jnp.mean(xf * xf, axis=-1, keepdims=True) + EPS)
    return (y * g.astype(jnp.float32)).astype(x.dtype)

def rope_tables(positions):
    inv = ROPE_THETA ** (-jnp.arange(0, ROT_DIM, 2, dtype=jnp.float32) / ROT_DIM)
    ang = positions.astype(jnp.float32)[..., None] * inv
    return jnp.cos(ang)[:, :, None, :], jnp.sin(ang)[:, :, None, :]

def partial_rope(x, cos, sin):
    xf = x.astype(jnp.float32)
    half = ROT_DIM // 2
    x1, x2, rest = xf[..., :half], xf[..., half:ROT_DIM], xf[..., ROT_DIM:]
    out = jnp.concatenate([x1 * cos - x2 * sin, x2 * cos + x1 * sin, rest], axis=-1)
    return out.astype(x.dtype)

def qk_prep(t, g, cos, sin):
    return partial_rope(rms_norm(t, g), cos, sin)

def banded_attention(q, k, v, max_rel, sinks=None):
    B, L, H, Dh = q.shape
    Hk = k.shape[2]
    rep = H // Hk
    nb = L // BLK
    qb = q.reshape(B, nb, BLK, Hk, rep, Dh)
    kb = k.reshape(B, nb, BLK, Hk, Dh)
    vb = v.reshape(B, nb, BLK, Hk, Dh)
    pad = ((0, 0), (1, 0), (0, 0), (0, 0), (0, 0))
    kk = jnp.concatenate([jnp.pad(kb, pad)[:, :-1], kb], axis=2)
    vv = jnp.concatenate([jnp.pad(vb, pad)[:, :-1], vb], axis=2)
    s = jnp.einsum('bnqgrd,bnkgd->bngrqk', qb, kk,
                   preferred_element_type=jnp.float32) * (Dh ** -0.5)
    i = jnp.arange(BLK)[:, None]
    j = jnp.arange(2 * BLK)[None, :]
    rel = BLK + i - j
    kpos = jnp.arange(nb)[:, None, None] * BLK + j[None] - BLK
    mask = ((rel >= 0) & (rel <= max_rel))[None] & (kpos >= 0)
    s = jnp.where(mask[None, :, None, None], s, -jnp.inf)
    m = jnp.max(s, axis=-1, keepdims=True)
    if sinks is not None:
        sk = sinks.astype(jnp.float32).reshape(1, 1, Hk, rep, 1, 1)
        m = jnp.maximum(m, sk)
    p = jnp.exp(s - m)
    denom = jnp.sum(p, axis=-1, keepdims=True)
    if sinks is not None:
        denom = denom + jnp.exp(sk - m)
    o = jnp.einsum('bngrqk,bnkgd->bnqgrd', (p / denom).astype(v.dtype), vv)
    lse = (m + jnp.log(denom))[..., 0]
    lse = lse.transpose(0, 1, 4, 2, 3).reshape(B, L, H)
    return o.reshape(B, L, H, Dh), lse

def dilated_attention(q, k, v):
    B, S, _, Dh = q.shape
    outs, lses = [], []
    for g, (window, dil) in enumerate(DIL_GROUPS):
        hs = slice(g * DIL_HPG, (g + 1) * DIL_HPG)
        L = S // dil
        Lp = -(-L // BLK) * BLK

        def to_sub(t):
            t = t[:, :, hs].reshape(B, L, dil, DIL_HPG, Dh).transpose(0, 2, 1, 3, 4)
            t = t.reshape(B * dil, L, DIL_HPG, Dh)
            return jnp.pad(t, ((0, 0), (0, Lp - L), (0, 0), (0, 0)))

        o, lse = banded_attention(to_sub(q), to_sub(k), to_sub(v), window // dil)
        o = o[:, :L].reshape(B, dil, L, DIL_HPG, Dh).transpose(0, 2, 1, 3, 4).reshape(B, S, DIL_HPG, Dh)
        lse = lse[:, :L].reshape(B, dil, L, DIL_HPG).transpose(0, 2, 1, 3).reshape(B, S, DIL_HPG)
        outs.append(o)
        lses.append(lse)
    alpha = jax.nn.softmax(jnp.stack(lses), axis=0)
    return jnp.einsum('gbsh,gbshd->bshd', alpha.astype(q.dtype), jnp.stack(outs))

def spatial_gating(u, v, g_norm, w_s, b_s):
    B, S, _ = u.shape
    u = jax.nn.gelu(u)
    v = rms_norm(jax.nn.gelu(v), g_norm)
    vc = v.reshape(B, S // SGU_CHUNK, SGU_CHUNK, SGU_GROUPS, HEAD_DIM)
    w = w_s * jnp.tril(jnp.ones((SGU_CHUNK, SGU_CHUNK), dtype=w_s.dtype))
    s = jnp.einsum('gts,bcsgd->bctgd', w, vc) + b_s.T[:, :, None]
    return u * s.reshape(B, S, SGU_WIDTH)

def even_mixer(h, cos, sin, w_in, w_out, sgu_norm, sgu_w, sgu_b, qn, kn):
    B, S, _ = h.shape
    u, v, q, k, val = jnp.split(h @ w_in, EVEN_SPLITS, axis=-1)
    a = spatial_gating(u, v, sgu_norm, sgu_w, sgu_b)
    q = qk_prep(q.reshape(B, S, DIL_HEADS, HEAD_DIM), qn, cos, sin)
    k = qk_prep(k.reshape(B, S, DIL_HEADS, HEAD_DIM), kn, cos, sin)
    b = dilated_attention(q, k, val.reshape(B, S, DIL_HEADS, HEAD_DIM)).reshape(B, S, -1)
    return jnp.concatenate([a, b], axis=-1) @ w_out

def odd_mixer(h, cos, sin, w_in, w_out, qn, kn, sinks):
    B, S, _ = h.shape
    q, k, v = jnp.split(h @ w_in, ODD_SPLITS, axis=-1)
    q = qk_prep(q.reshape(B, S, SWA_Q_HEADS, HEAD_DIM), qn, cos, sin)
    k = qk_prep(k.reshape(B, S, SWA_KV_HEADS, HEAD_DIM), kn, cos, sin)
    v = v.reshape(B, S, SWA_KV_HEADS, HEAD_DIM)
    o, _ = banded_attention(q, k, v, SWA_WINDOW - 1, sinks)
    return o.reshape(B, S, -1) @ w_out

def hier_moe(h, w_rg, b_rg, w_re, b_re, w_gate, w_up, w_down):
    B, S, D = h.shape
    T = B * S
    x = h.reshape(T, D)
    xf = x.astype(jnp.float32)
    lg = xf @ w_rg.astype(jnp.float32) + b_rg.astype(jnp.float32)
    gi = jnp.argmax(lg, axis=-1)
    p_top = jnp.take_along_axis(jax.nn.softmax(lg, axis=-1), gi[:, None], axis=-1)
    le = jnp.einsum('td,gde->tge', xf, w_re.astype(jnp.float32)) + b_re.astype(jnp.float32)
    idx = jnp.broadcast_to(gi[:, None, None], (T, 1, EXPERTS_PER_GROUP))
    le = jnp.take_along_axis(le, idx, axis=1)[:, 0]
    top_p, top_i = lax.top_k(jax.nn.softmax(le, axis=-1), TOP_K)
    gate = p_top * top_p / jnp.sum(top_p, axis=-1, keepdims=True)
    eid = gi[:, None] * EXPERTS_PER_GROUP + top_i

    P = T * TOP_K
    flat_e = eid.reshape(-1)
    flat_tok = jnp.repeat(jnp.arange(T, dtype=jnp.int32), TOP_K)
    order = jnp.argsort(flat_e)
    se, stok, sw = flat_e[order], flat_tok[order], gate.reshape(-1)[order]
    counts = jnp.bincount(flat_e, length=N_EXPERTS)
    padded = (counts + MOE_BLOCK - 1) // MOE_BLOCK * MOE_BLOCK
    pad_end = jnp.cumsum(padded)
    pad_start = pad_end - padded
    start = jnp.cumsum(counts) - counts
    dest = pad_start[se] + (jnp.arange(P) - start[se])
    R = P + N_EXPERTS * MOE_BLOCK
    nblk = R // MOE_BLOCK
    buf = jnp.zeros((R, D), x.dtype).at[dest].set(x[stok])
    blk_e = jnp.clip(jnp.searchsorted(pad_end, jnp.arange(nblk) * MOE_BLOCK, side='right'),
                     0, N_EXPERTS - 1)

    def run_block(args):
        xb, e = args
        hid = jax.nn.silu(xb @ w_gate[e]) * (xb @ w_up[e])
        return hid @ w_down[e]

    out = lax.map(run_block, (buf.reshape(nblk, MOE_BLOCK, D), blk_e)).reshape(R, D)
    y = jax.ops.segment_sum(out[dest] * sw[:, None].astype(out.dtype), stok, num_segments=T)
    return y.reshape(B, S, D)

def setup_inputs(seed: int = 0) -> dict:
    key = jax.random.key(seed)
    ks = jax.random.split(key, 24)
    f32 = jnp.float32

    def nrm(k, shape, scale):
        return jax.random.normal(k, shape, f32) * scale

    def gain(k, shape):
        return 1.0 + 0.02 * jax.random.normal(k, shape, f32)

    x = jax.random.normal(ks[0], (BATCH, SEQ, D_MODEL), f32)
    positions = jnp.broadcast_to(jnp.arange(SEQ, dtype=jnp.int32), (BATCH, SEQ))
    return {
        "x": x,
        "positions": positions,
        "norm_mix": gain(ks[1], (DEPTH, D_MODEL)),
        "norm_ffn": gain(ks[2], (DEPTH, D_MODEL)),
        "w_in_even": nrm(ks[3], (N_EVEN, D_MODEL, IN_EVEN), D_MODEL ** -0.5),
        "w_out_even": nrm(ks[4], (N_EVEN, OUT_EVEN, D_MODEL), OUT_EVEN ** -0.5),
        "sgu_norm": gain(ks[5], (N_EVEN, SGU_WIDTH)),
        "sgu_w": nrm(ks[6], (N_EVEN, SGU_GROUPS, SGU_CHUNK, SGU_CHUNK), SGU_CHUNK ** -0.5),
        "sgu_b": 1.0 + 0.1 * jax.random.normal(ks[7], (N_EVEN, SGU_GROUPS, SGU_CHUNK), f32),
        "qn_dil": gain(ks[8], (N_EVEN, HEAD_DIM)),
        "kn_dil": gain(ks[9], (N_EVEN, HEAD_DIM)),
        "w_in_odd": nrm(ks[10], (N_ODD, D_MODEL, IN_ODD), D_MODEL ** -0.5),
        "w_out_odd": nrm(ks[11], (N_ODD, OUT_ODD, D_MODEL), OUT_ODD ** -0.5),
        "qn_swa": gain(ks[12], (N_ODD, HEAD_DIM)),
        "kn_swa": gain(ks[13], (N_ODD, HEAD_DIM)),
        "sinks": nrm(ks[14], (N_ODD, SWA_Q_HEADS), 0.5),
        "w_router_g": nrm(ks[15], (DEPTH, D_MODEL, N_GROUPS), D_MODEL ** -0.5),
        "b_router_g": nrm(ks[16], (DEPTH, N_GROUPS), 0.01),
        "w_router_e": nrm(ks[17], (DEPTH, N_GROUPS, D_MODEL, EXPERTS_PER_GROUP), D_MODEL ** -0.5),
        "b_router_e": nrm(ks[18], (DEPTH, N_GROUPS, EXPERTS_PER_GROUP), 0.01),
        "w_gate": nrm(ks[19], (DEPTH, N_EXPERTS, D_MODEL, EXPERT_FF), D_MODEL ** -0.5),
        "w_up": nrm(ks[20], (DEPTH, N_EXPERTS, D_MODEL, EXPERT_FF), D_MODEL ** -0.5),
        "w_down": nrm(ks[21], (DEPTH, N_EXPERTS, EXPERT_FF, D_MODEL), EXPERT_FF ** -0.5),
    }

def reference(x, positions, norm_mix, norm_ffn, w_in_even, w_out_even, sgu_norm, sgu_w, sgu_b,
              qn_dil, kn_dil, w_in_odd, w_out_odd, qn_swa, kn_swa, sinks,
              w_router_g, b_router_g, w_router_e, b_router_e, w_gate, w_up, w_down):
    cos, sin = rope_tables(positions)
    h = x
    for layer in range(DEPTH):
        i = layer // 2
        hn = rms_norm(h, norm_mix[layer])
        if layer % 2 == 0:
            h = h + even_mixer(hn, cos, sin, w_in_even[i], w_out_even[i], sgu_norm[i],
                               sgu_w[i], sgu_b[i], qn_dil[i], kn_dil[i])
        else:
            h = h + odd_mixer(hn, cos, sin, w_in_odd[i], w_out_odd[i], qn_swa[i], kn_swa[i],
                              sinks[i])
        h = h + hier_moe(rms_norm(h, norm_ffn[layer]), w_router_g[layer], b_router_g[layer],
                         w_router_e[layer], b_router_e[layer], w_gate[layer], w_up[layer],
                         w_down[layer])
    return h


_drawn_inputs = setup_inputs


def setup_inputs(seed=0):
    import zlib

    import numpy as np

    out = dict(_drawn_inputs(seed))
    spreads = {}
    factors = {'sgu_norm': 2.764,
     'qn_dil': 5.533,
     'kn_dil': 6.302,
     'qn_swa': 6.319,
     'kn_swa': 8.0,
     'sinks': 200.0,
     'b_router_g': 3.314}
    for name, (base, spread) in spreads.items():
        noise = np.random.default_rng([zlib.crc32(name.encode()), seed]).standard_normal(out[name].shape)
        drawn = base * np.exp(spread * noise) if base else spread * noise
        out[name] = __import__('jax').numpy.asarray(drawn.astype(out[name].dtype))
    for name, factor in factors.items():
        out[name] = (out[name] * factor).astype(out[name].dtype)
    return out
```

```python
import concourse.bass as bass
from concourse import mybir
from contextlib import ExitStack, contextmanager
import numpy as np

F32 = mybir.dt.float32
BF16 = mybir.dt.bfloat16
I32 = mybir.dt.int32
ACT = mybir.ActivationFunctionType
ALU = mybir.AluOpType
AX = mybir.AxisListType.X

P = 128
T = 2048
D = 1024
DK = D // P
NT = T // P
HD = 64
ROT = HD // 4
HALF = ROT // 2
THETA = 500000.0
EPS = 1e-6
SCALE = HD ** -0.5
SGU = 512
SG = 8
DIL = ((1, 16), (4, 4), (16, 1))
NDH = 12
DW = NDH * HD
QUAD = 4 * HD
GROUPS, EPG = 4, 8
NE = GROUPS * EPG
FF = 256
NL = GROUPS + NE
NBMAX = 68
NEG = -1e30
BIG = 1e6


IN0_PARTS = ((0, 1024), (1024, 768), (1792, 768), (2560, 768))


class Count:

    def __init__(self, sem, credit=0):
        self.sem, self.credit = sem, credit


class Step:

    def __init__(self, i, j, u):
        self.i, self.j, self.u = i, j, u
        self.n = i * u + j

    def within(self, total):
        return not isinstance(self.n, int) or self.n < total

    def plus(self, k):
        q, j = divmod(self.j + k, self.u)
        return Step(self.i + q, j, self.u)

    def slot(self, m):
        return self.j % m

    def turn(self, m):
        return self.i * (self.u // m) + self.j // m


def until(eng, count, k):
    eng.wait_ge(count.sem, k + count.credit)


def alone(eng, count, k, tick):
    eng.wait_ge(count.sem, k + count.credit)
    eng.sem_inc(tick, 1)


class Chain:

    def __init__(self, eng, sem, tick=None):
        self.eng, self.sem, self.tick = eng, sem, tick
        self.base, self.n = 0, 0

    def link(self, ins):
        ins.then_inc(self.sem, 1)
        self.n += 1
        self.eng.wait_ge(self.sem, self.base + self.n)
        if self.tick is not None:
            self.eng.sem_inc(self.tick, 1)

    def mark(self, ins):
        ins.then_inc(self.sem, 1)
        self.n += 1

    def meet(self):
        self.eng.wait_ge(self.sem, self.base + self.n)
        if self.tick is not None:
            self.eng.sem_inc(self.tick, 1)


def looped(eng, total, u, tail, step, chain=None, per=0):
    rounds = (total - tail) // u
    start = chain.base + chain.n if chain else 0
    with eng.Fori(0, rounds) as i:
        if chain:
            chain.base, chain.n = i * (per * u) + start, 0
        for j in range(u):
            step(Step(i, j, u))
        if chain:
            assert chain.n == per * u, f"the chain has {chain.n / u} links a step"
    if chain:
        chain.base, chain.n = start + rounds * per * u, 0
    for n in range(rounds * u, total):
        step(Step(n // u, n % u, u))


def rows(ap, n):
    v = ap.rearrange("(n p) c -> n p c", p=P)
    if isinstance(n, int):
        return v[n]
    return v[bass.ds(n, 1)].rearrange("a p c -> (a p) c")


class Kernel:
    def __init__(self, nc, ins, out):
        self.nc, self.x, self.out = nc, ins, out
        self.ctx = ExitStack()

    def dram(self, name, shape, dt=F32):
        return self.nc.dram_tensor(name, shape, dt).ap()

    @contextmanager
    def phase(self, name):
        sems = []
        with ExitStack() as s:
            def sb(n, shape, dt=F32):
                return s.enter_context(self.nc.sbuf_tensor(f"{name}_{n}", shape, dt))

            def sem(n):
                sems.append(self.nc.alloc_semaphore(name=f"{name}_{n}"))
                return sems[-1]

            yield sb, sem, s.enter_context(self.nc.Block())
        self.nc.clear_and_free_semaphores(sems)
        self.nc.all_engine_barrier()

    def build(self):
        nc = self.nc
        with self.ctx:
            keep = lambda n, shape, dt=F32: self.ctx.enter_context(nc.sbuf_tensor(n, shape, dt))
            self.ident = keep("ident", [P, P])
            self.identb = keep("identb", [P, P], BF16)
            self.masks = keep("masks", [P, 3, 2 * P], BF16)
            self.before = keep("before", [P, P], BF16)
            self.onesb = keep("onesb", [P, P], BF16)
            self.weights = keep("weights", [P, DK * 3328])
            self.expert_w = keep("expert_w", [P, 2, DK * 2 * FF + 2 * D])
            self.who = keep("who", [P, NBMAX], I32)
            self.where = keep("where", [P, NBMAX], I32)
            self.gates = keep("gates", [P, NBMAX])
            self.ends_i = keep("ends_i", [1, NE + 1], I32)
            self.ps = self.ctx.enter_context(nc.psum_tensor("ps", [P, 4096], F32))
            self.tick = self.ctx.enter_context(nc.semaphore("tick_pool"))
            self.tick_pe = self.ctx.enter_context(nc.semaphore("tick_pe"))
            self.tick_sp = self.ctx.enter_context(nc.semaphore("tick_sp"))
            self.weights_in = [self.ctx.enter_context(nc.semaphore(f"weights_in{i}")) for i in range(7)]
            self.expert_in = [[self.ctx.enter_context(nc.semaphore(f"expert_in{l}{i}")) for i in range(2)]
                              for l in range(2)]
            self.rope_d = self.dram("rope_d", [T, ROT])
            self.q_d = self.dram("q_d", [T, D])
            self.k_d = self.dram("k_d", [T, DW])
            self.v_d = self.dram("v_d", [T, DW])
            self.a_d = self.dram("a_d", [T, SGU])
            self.o_d = self.dram("o_d", [T, 3 * (QUAD + 8)])
            self.k1_d = self.dram("k1_d", [T, 4 * HD])
            self.v1_d = self.dram("v1_d", [T, 2 * HD])
            self.o1_d = self.dram("o1_d", [T, D])
            self.h_d = [self.dram("h_d", [T + P, D]), self.out]
            self.hn_d = [self.dram(f"hn{i}_d", [T, D]) for i in range(2)]
            self.lg_d = [self.dram(f"lg{i}_d", [T, NL]) for i in range(2)]
            w = self.weights
            self.w_in0 = w[:, :].rearrange("p (k n) -> p k n", k=DK)
            self.w_out0 = w[:, 0:6 * D].rearrange("p (k n) -> p k n", k=6)
            self.w_in1 = w[:, 6 * D:6 * D + DK * 1280].rearrange("p (k n) -> p k n", k=DK)
            self.w_out1 = w[:, 16 * D:24 * D].rearrange("p (k n) -> p k n", k=DK)
            setup(self)
            project_in(self, 0)
            attend(self, 0)
            project_out(self, 0)
            route(self, 0)
            experts(self, 0)
            project_in(self, 1)
            attend(self, 1)
            project_out(self, 1)
            route(self, 1)
            experts(self, 1)


def setup(K):
    nc, ps = K.nc, K.ps
    with K.phase("s") as (sb, sem, block):
        pos_i = sb("pos_i", [P, NT], I32)
        pos = sb("pos", [P, NT])
        inv = sb("inv", [P, HALF])
        ang = sb("ang", [P, NT, HALF])
        turns = sb("turns", [P, NT, HALF])
        rest = sb("rest", [P, NT, HALF])
        table = sb("table", [P, NT, ROT])
        quarter = sb("quarter", [P, 1])
        pos_in, own, tab, sin_done, stored, made = (sem(n) for n in
            ("pos_in", "own", "tab", "sin_done", "stored", "made"))
        pool_own = sem("pool_own")

        @block.sync
        def _(sp):
            with nc.allow_non_contiguous_dma("2048 positions, once"):
                sp.dma_start(pos_i[:, :], K.x["positions"].rearrange("a (n p) -> p (a n)", p=P)).then_inc(pos_in, 16)
            for n, (c0, wd) in enumerate(IN0_PARTS):
                sp.dma_start(K.w_in0[:, :, c0:c0 + wd],
                             K.x["w_in_even"].rearrange("a (p k) n -> p (a k) n", k=DK)[:, :, c0:c0 + wd]
                             ).then_inc(K.weights_in[(0, 4, 5, 6)[n]], 16)
            sp.wait_ge(made, 1)
            for h in K.h_d:
                sp.dma_start(h[T:T + P, :], K.expert_w[:, 0, 0:D]).then_inc(stored, 16)
            sp.wait_ge(sin_done, 2)
            sp.dma_start(K.rope_d.rearrange("(n p) c -> p n c", p=P), table[:, :, :]).then_inc(stored, 16)
            sp.wait_ge(stored, 48)

        @block.gpsimd
        def _(g):
            own_ = Chain(g, pool_own)
            for t in (K.ident, K.identb):
                own_.link(g.memset(t[:, :], 0.0))
                own_.link(g.affine_select(out=t[:, :], in_=t[:, :], compare_op=ALU.not_equal, fill=1.0,
                                          base=0, pattern=[[-1, P]], channel_multiplier=1))
            own_.link(g.memset(K.masks[:, :, :], 0.0))
            for m, (base, mult) in enumerate(((0, -1), (-1, -1), (-P, 0))):
                for b, c, s in ((base, mult, 1), (P, 1, -1)):
                    own_.link(g.affine_select(out=K.masks[:, m, :], in_=K.masks[:, m, :], compare_op=ALU.is_ge,
                                              fill=NEG, base=b, pattern=[[s, 2 * P]], channel_multiplier=c))
            own_.link(g.memset(K.onesb[:, :], 1.0))
            own_.link(g.affine_select(out=K.before[:, :], in_=K.onesb[:, :], compare_op=ALU.is_ge, fill=0.0,
                                      base=-1, pattern=[[1, P]], channel_multiplier=-1))
            own_.link(g.memset(K.expert_w[:, 0, 0:D], 0.0))
            g.sem_inc(made, 1)

        @block.vector
        def _(v):
            own_ = Chain(v, own)
            v.wait_ge(pos_in, 16)
            own_.link(nc.vector.tensor_copy(pos[:, :], pos_i[:, :]))
            own_.link(nc.vector.memset(quarter[:, :], np.pi / 2))
            for c in range(HALF):
                own_.link(nc.vector.memset(inv[:, c:c + 1], float(np.float32(THETA) ** np.float32(-2.0 * c / ROT))))
            shape = [P, NT, HALF]
            own_.link(nc.vector.tensor_tensor(ang[:, :, :], pos[:, :].unsqueeze(2).broadcast_to(shape),
                                              inv[:, :].unsqueeze(1).broadcast_to(shape), ALU.mult))
            magic = 1.5 * 2.0 ** 23
            own_.link(nc.vector.tensor_scalar(turns[:, :, :], ang[:, :, :], float(1 / (2 * np.pi)), magic, ALU.mult, ALU.add))
            own_.link(nc.vector.tensor_scalar(turns[:, :, :], turns[:, :, :], magic, None, ALU.subtract))
            own_.link(nc.vector.tensor_copy(rest[:, :, :], ang[:, :, :]))
            left = 2 * np.pi
            for bits in (7, 16, 25, 60):
                part = np.floor(left * 2.0 ** bits) / 2.0 ** bits if bits < 60 else left
                left -= part
                own_.link(nc.vector.scalar_tensor_tensor(rest[:, :, :], turns[:, :, :], -float(part), rest[:, :, :],
                                                         ALU.mult, ALU.add))
            own_.link(nc.vector.tensor_scalar(rest[:, :, :], rest[:, :, :], 3.1415925, -3.1415925, ALU.min, ALU.max))
            nc.vector.scalar_tensor_tensor(ang[:, :, :], rest[:, :, :], -1.0, rest[:, :, :], ALU.mult, ALU.max).then_inc(tab, 1)

        @block.scalar
        def _(a):
            a.wait_ge(tab, 1)
            nc.scalar.activation(table[:, :, 0:HALF], ang[:, :, :], ACT.Sin, scale=-1.0, bias=quarter[:, 0:1]).then_inc(sin_done, 1)
            nc.scalar.activation(table[:, :, HALF:ROT], rest[:, :, :], ACT.Sin).then_inc(sin_done, 1)


def project_in(K, layer):
    nc, ps = K.nc, K.ps
    even = layer == 0
    w = K.w_in0 if even else K.w_in1
    NQK = 2 * NDH if even else 18
    QKW = NQK * HD
    if even:
        groups = [(0, 512), (512, 512), (1024, 384), (1408, 384), (1792, 384), (2176, 384), (2560, 384), (2944, 384)]
        ring, by_act = 4, 6
    else:
        groups = [(0, 512), (512, 512), (1024, 256)]
        ring, by_act = 3, 3
    by_dve = len(groups) - by_act
    nb = 1 if even else 2

    with K.phase(f"in{layer}") as (sb, sem, block):
        xt = sb("xt", [P, 2, D])
        cs = sb("cs", [P, 2, ROT])
        xn = sb("xn", [P, D])
        junk = sb("junk", [P, D], BF16)
        hnT = sb("hnT", [P, 2, DK, P])
        gain = sb("gain", [P, DK])
        qk_gain = sb("qk_gain", [P, 2, HD])
        qk_ = sb("qk", [P, nb, QKW])
        sq = sb("sq", [P, QKW])
        ssx, rx = sb("ssx", [P, 2]), sb("rx", [P, 2])
        ssq, rq = sb("ssq", [P, NQK]), sb("rq", [P, NQK])
        rot = sq[:, 0:4 * NQK * HALF].rearrange("p (r h c) -> p r h c", r=4, h=NQK)
        power = sb("power", [P, 1])
        if even:
            u, v = sb("u", [P, SGU]), sb("v", [P, SGU])
            av = sb("av", [P, SGU])
            v_gain = sb("v_gain", [P, SGU])
            ssv, rv = sb("ssv", [P, 1]), sb("rv", [P, 1])
            ws = sb("ws", [P, SG, P])
            bs, bsT = sb("bs", [SG, P]), sb("bsT", [P, SG])
        val_ = sb("val", [P, nb, DW if even else 2 * HD])
        x_in, cs_in = [sem("x_in0"), sem("x_in1")], [sem("cs_in0"), sem("cs_in1")]
        par_in, st, own, pool_own = sem("par_in"), sem("st"), sem("own"), sem("pool_own")
        xn_done, roped = Count(sem("xn_done"), 2), Count(sem("roped"), 2)
        sum_x, rms_x = Count(sem("sum_x"), 1), Count(sem("rms_x"), 2)
        sum_q, rms_q = Count(sem("sum_q")), Count(sem("rms_q"))
        sum_v, rms_v = Count(sem("sum_v")), Count(sem("rms_v"))
        turned, turned_out = Count(sem("turned"), 1), Count(sem("turned_out"), 1)
        grp, act_out, dve_out = Count(sem("grp")), Count(sem("act_out"), by_act), Count(sem("dve_out"), max(by_dve, 1))
        stored = Count(sem("stored"), nb)
        vn_done, mixed, gated = Count(sem("vn_done")), Count(sem("mixed")), Count(sem("gated"), 1)
        ready, power_set = sem("ready"), sem("power_set")
        ws_turned, ws_out = sem("ws_turned"), sem("ws_out")
        tp = ps[:, 0:D]
        mix = ps[:, 3072:3072 + SGU]

        def bank(gi):
            return ps[:, 1024 + 512 * (gi % ring):1024 + 512 * (gi % ring) + groups[gi][1]]

        @block.sync
        def _(sp):
            sp.wait_ge(ready, 1)
            sp.dma_start(gain[:, :], K.x["norm_mix"][layer].rearrange("(p k) -> p k", k=DK)).then_inc(par_in, 16)
            names = ("qn_dil", "kn_dil") if even else ("qn_swa", "kn_swa")
            for i, name in enumerate(names):
                sp.dma_start(qk_gain[:, i, :], K.x[name].broadcast_to([P, HD])).then_inc(par_in, 16)
            if even:
                sp.dma_start(v_gain[:, :], K.x["sgu_norm"].broadcast_to([P, SGU])).then_inc(par_in, 16)
                sp.dma_start(ws[:, :, :], K.x["sgu_w"].rearrange("a g t c -> t (a g) c")).then_inc(par_in, 16)
                sp.dma_start(bs[:, :], K.x["sgu_b"].rearrange("a g t -> (a g) t")).then_inc(par_in, 16)

            def load(s):
                j, n = s.slot(2), s.n
                alone(sp, xn_done, n - 1, K.tick_sp)
                src = K.x["x"].rearrange("a t c -> (a t) c") if even else K.h_d[0][0:T]
                sp.dma_start(xt[:, j, :], rows(src, n)).then_inc(x_in[j], 16)

            def load_cs(s):
                sp.dma_start(cs[:, s.slot(2), :], rows(K.rope_d, s.n)).then_inc(cs_in[s.slot(2)], 16)

            def store(s):
                b, n = s.slot(2) % nb, s.n
                alone(sp, roped, n + 1, K.tick_sp)
                if even:
                    alone(sp, gated, n + 1, K.tick_sp)
                    sp.dma_start(rows(K.q_d[:, 0:DW], n), qk_[:, b, 0:DW]).then_inc(st, 16)
                    sp.dma_start(rows(K.k_d, n), qk_[:, b, DW:2 * DW]).then_inc(st, 16)
                    sp.dma_start(rows(K.v_d, n), val_[:, b, :]).then_inc(st, 16)
                    sp.dma_start(rows(K.a_d, n), av[:, :]).then_inc(st, 16)
                else:
                    sp.dma_start(rows(K.q_d, n), qk_[:, b, 0:D]).then_inc(st, 16)
                    for dup in range(2):
                        sp.dma_start(rows(K.k1_d, n).rearrange("p (h d c) -> p h d c", h=2, d=2)[:, :, dup, :],
                                     qk_[:, b, D:D + 2 * HD].rearrange("p (h c) -> p h c", h=2)).then_inc(st, 16)
                    sp.dma_start(rows(K.v1_d, n), val_[:, b, :]).then_inc(st, 16)

            def step(s):
                if s.plus(2).within(NT):
                    load(s.plus(2))
                store(s)
                if s.plus(2).within(NT):
                    load_cs(s.plus(2))
                sp.wait_ge(st, s.n * 64 + 64)
                sp.sem_inc(stored.sem, 1)
            sp.sem_inc(stored.sem, stored.credit)
            for s in (Step(0, 0, 2), Step(0, 1, 2)):
                load(s)
                load_cs(s)
            looped(sp, NT, 2, 2, step)

        @block.scalar
        def _(a):
            def square(s):
                j = s.slot(2)
                until_x(a, s)
                until(a, rms_x, s.n - 1)
                until(a, sum_x, s.n)
                nc.scalar.activation(junk[:, :], xt[:, j, :], ACT.Square, accum_out=ssx[:, j:j + 1]).then_inc(sum_x.sem, 1)

            def until_x(eng, s):
                eng.wait_ge(x_in[s.slot(2)], s.turn(2) * 16 + 16)

            def step(s):
                if s.plus(1).within(NT):
                    square(s.plus(1))
                if even:
                    until(a, gated, s.n)
                for gi, (c0, wd) in enumerate(groups[:by_act]):
                    until(a, grp, s.n * len(groups) + gi + 1)
                    if even and gi < 2:
                        nc.scalar.activation((u, v)[gi][:, :], bank(gi), ACT.Gelu_apprx_tanh).then_inc(act_out.sem, 1)
                        continue
                    if gi == (2 if even else 0):
                        until(a, stored, s.n - nb + 1)
                    b = s.slot(2) % nb
                    qk, val = qk_[:, b, :], val_[:, b, :]
                    q0 = c0 - (1024 if even else 0)
                    if not even and gi == 2:
                        nc.scalar.activation(qk[:, D:D + 2 * HD], bank(gi)[:, 0:2 * HD], ACT.Copy)
                        nc.scalar.activation(val, bank(gi)[:, 2 * HD:4 * HD], ACT.Copy).then_inc(act_out.sem, 1)
                    else:
                        nc.scalar.activation(qk[:, q0:q0 + wd], bank(gi), ACT.Copy).then_inc(act_out.sem, 1)
            a.sem_inc(act_out.sem, act_out.credit)
            a.sem_inc(sum_x.sem, sum_x.credit)
            square(Step(0, 0, 2))
            looped(a, NT, 2, 2, step)

        @block.gpsimd
        def _(g):
            own_ = Chain(g, pool_own)
            own_.link(g.memset(power[:, :], -0.5))
            g.sem_inc(rms_x.sem, rms_x.credit)
            if even:
                g.wait_ge(ws_out, SG)
                own_.link(g.affine_select(out=ws[:, :, :], in_=ws[:, :, :], compare_op=ALU.is_ge, fill=0.0,
                                          base=0, pattern=[[0, SG], [1, P]], channel_multiplier=-1))
            g.sem_inc(power_set, 1)

            def rms(own_, out, total, width, done):
                own_.link(g.tensor_scalar(out, total, 1.0 / width, EPS, ALU.mult, ALU.add))
                g.tensor_tensor(out, out, power[:, 0:1].broadcast_to([P, out.shape[1]]), ALU.pow).then_inc(done.sem, 1)

            def rms_tile(s):
                j = s.slot(2)
                alone(g, sum_x, s.n + 1, K.tick)
                alone(g, xn_done, s.n - 1, K.tick)
                rms(own_, rx[:, j:j + 1], ssx[:, j:j + 1], D, rms_x)

            def step(s):
                if s.plus(1).within(NT):
                    rms_tile(s.plus(1))
                if even:
                    alone(g, sum_v, s.n + 1, K.tick)
                    rms(own_, rv[:, :], ssv[:, :], SGU, rms_v)
                alone(g, sum_q, s.n + 1, K.tick)
                rms(own_, rq[:, :], ssq[:, :], HD, rms_q)
            rms_tile(Step(0, 0, 2))
            looped(g, NT, 2, 2, step,
                   own_, 2 + (1 if even else 0))

        @block.tensor
        def _(pe):
            def turn(s):
                j = s.slot(2)
                until(pe, xn_done, s.n + 1)
                until(pe, turned_out, s.n)
                src = xn[:, :].rearrange("p (c k) -> p k c", k=DK)
                for k in range(DK):
                    last = nc.tensor.transpose(tp[:, k * P:(k + 1) * P], src[:, k, :], K.ident[:, :])
                last.then_inc(turned.sem, 1)

            def group(s, gi):
                c0, wd = groups[gi]
                prev = gi - ring if gi >= ring else gi - ring + len(groups)
                n = s.n if gi >= ring else s.n - 1
                if prev < by_act:
                    until(pe, act_out, n * by_act + prev + 1)
                else:
                    until(pe, dve_out, n * by_dve + prev - by_act + 1)
                part = sum(c0 >= p0 for p0, _ in IN0_PARTS) - 1
                pe.wait_ge(K.weights_in[(0, 4, 5, 6)[part] if even else 2], 16)
                for k in range(DK):
                    last = nc.tensor.matmul(bank(gi), hnT[:, s.slot(2), k, :], w[:, k, c0:c0 + wd],
                                            start=(k == 0), stop=(k == DK - 1))
                last.then_inc(grp.sem, 1)

            def step(s):
                until(pe, turned_out, s.n + 1)
                cut = 6 if even else 2
                for gi in range(cut):
                    group(s, gi)
                if s.plus(1).within(NT):
                    turn(s.plus(1))
                for gi in range(cut, len(groups)):
                    group(s, gi)
                if even:
                    until(pe, vn_done, s.n + 1)
                    until(pe, gated, s.n)
                    for c in range(SG):
                        mm = nc.tensor.matmul(mix[:, c * HD:(c + 1) * HD], ws[:, c, :], v[:, c * HD:(c + 1) * HD],
                                              start=True, stop=True)
                    mm.then_inc(mixed.sem, 1)
            pe.sem_inc(turned.sem, turned.credit)
            if even:
                pe.wait_ge(par_in, 16 * 6)
                for c in range(SG):
                    nc.tensor.transpose(ps[:, 1024 + c * P:1024 + (c + 1) * P], ws[:, c, :], K.ident[:, :]).then_inc(ws_turned, 1)
                nc.tensor.transpose(ps[:, 3072:3072 + SG], bs[:, :], K.ident[0:SG, 0:SG]).then_inc(ws_turned, 1)
                pe.wait_ge(ws_out, SG + 1)
                pe.wait_ge(power_set, 1)
            turn(Step(0, 0, 2))
            looped(pe, NT, 2, 2, step)

        @block.vector
        def _(v_):
            own_ = Chain(v_, own)
            for c in (xn_done, roped, gated, turned_out):
                v_.sem_inc(c.sem, c.credit)
            v_.sem_inc(dve_out.sem, dve_out.credit)
            v_.sem_inc(ready, 1)
            v_.wait_ge(par_in, 16 * (6 if even else 3))
            if even:
                v_.wait_ge(ws_turned, SG + 1)
                for c in range(SG):
                    nc.vector.tensor_copy(ws[:, c, :], ps[:, 1024 + c * P:1024 + (c + 1) * P]).then_inc(ws_out, 1)
                nc.vector.tensor_copy(bsT[:, :], ps[:, 3072:3072 + SG]).then_inc(ws_out, 1)
            NQ = NQK // 2 if even else 16

            def norm(s):
                j = s.slot(2)
                until(v_, rms_x, s.n + 1)
                until(v_, turned, s.n)
                nc.vector.tensor_scalar(xn[:, :], xt[:, j, :], rx[:, j:j + 1], None, ALU.mult).then_inc(xn_done.sem, 1)

            def turn_out(s):
                until(v_, turned, s.n + 1)
                nc.vector.tensor_tensor(hnT[:, s.slot(2), :, :], tp.rearrange("p (k c) -> p k c", k=DK),
                                        gain[:, :].unsqueeze(2).broadcast_to([P, DK, P]), ALU.mult).then_inc(turned_out.sem, 1)

            def step(s):
                if even:
                    until(v_, act_out, s.n * by_act + 2)
                    v_norm(s)
                if s.plus(1).within(NT):
                    norm(s.plus(1))
                    turn_out(s.plus(1))
                until(v_, act_out, s.n * by_act + by_act)
                qk, val = qk_[:, s.slot(2) % nb, :], val_[:, s.slot(2) % nb, :]
                heads = qk.rearrange("p (h c) -> p h c", c=HD)
                own_.link(nc.vector.tensor_tensor(sq[:, :], qk, qk, ALU.mult))
                nc.vector.tensor_reduce(ssq[:, :], sq[:, :].rearrange("p (h c) -> p h c", c=HD), AX, ALU.add).then_inc(sum_q.sem, 1)
                if even:
                    until(v_, stored, s.n)
                    for gi in (6, 7):
                        until(v_, grp, s.n * len(groups) + gi + 1)
                        nc.vector.tensor_copy(val[:, 384 * (gi - 6):384 * (gi - 5)], bank(gi)).then_inc(dve_out.sem, 1)
                until(v_, rms_q, s.n + 1)
                own_.link(nc.vector.tensor_tensor(heads, heads, rq[:, :].unsqueeze(2).broadcast_to([P, NQK, HD]), ALU.mult))
                own_.mark(nc.vector.tensor_tensor(heads[:, 0:NQ, :], heads[:, 0:NQ, :],
                                                  qk_gain[:, 0, :].unsqueeze(1).broadcast_to([P, NQ, HD]), ALU.mult))
                own_.link(nc.vector.tensor_tensor(heads[:, NQ:NQK, :], heads[:, NQ:NQK, :],
                                                  qk_gain[:, 1, :].unsqueeze(1).broadcast_to([P, NQK - NQ, HD]), ALU.mult))
                j = s.slot(2)
                v_.wait_ge(cs_in[j], s.turn(2) * 16 + 16)
                wide = [P, NQK, HALF]
                cos = cs[:, j, 0:HALF].unsqueeze(1).broadcast_to(wide)
                sin = cs[:, j, HALF:ROT].unsqueeze(1).broadcast_to(wide)
                x1, x2 = heads[:, :, 0:HALF], heads[:, :, HALF:ROT]
                own_.mark(nc.vector.tensor_tensor(rot[:, 0, :, :], x1, cos, ALU.mult))
                own_.mark(nc.vector.tensor_tensor(rot[:, 1, :, :], x2, sin, ALU.mult))
                own_.mark(nc.vector.tensor_tensor(rot[:, 2, :, :], x2, cos, ALU.mult))
                own_.link(nc.vector.tensor_tensor(rot[:, 3, :, :], x1, sin, ALU.mult))
                own_.mark(nc.vector.tensor_tensor(x1, rot[:, 0, :, :], rot[:, 1, :, :], ALU.subtract))
                own_.link(nc.vector.tensor_tensor(x2, rot[:, 2, :, :], rot[:, 3, :, :], ALU.add))
                v_.sem_inc(roped.sem, 1)
                if even:
                    until(v_, mixed, s.n + 1)
                    own_.link(nc.vector.tensor_tensor(av[:, :].rearrange("p (c d) -> p c d", c=SG),
                                                      mix.rearrange("p (c d) -> p c d", c=SG),
                                                      bsT[:, :].unsqueeze(2).broadcast_to([P, SG, HD]), ALU.add))
                    nc.vector.tensor_tensor(av[:, :], av[:, :], u[:, :], ALU.mult).then_inc(gated.sem, 1)

            def v_norm(s):
                until(v_, stored, s.n)
                own_.link(nc.vector.tensor_tensor(av[:, :], v[:, :], v[:, :], ALU.mult))
                nc.vector.tensor_reduce(ssv[:, :], av[:, :], AX, ALU.add).then_inc(sum_v.sem, 1)
                until(v_, rms_v, s.n + 1)
                nc.vector.scalar_tensor_tensor(v[:, :], v[:, :], rv[:, 0:1], v_gain[:, :], ALU.mult, ALU.mult).then_inc(vn_done.sem, 1)

            norm(Step(0, 0, 2))
            turn_out(Step(0, 0, 2))
            looped(v_, NT, 2, 2, step, own_,
                   12 if even else 10)



def attend(K, layer):
    nc, ps = K.nc, K.ps
    even = layer == 0
    U = 4
    N = 3 * NT if even else 4 * NT
    OW = QUAD + 8 if even else QUAD
    KH = 4 if even else 2
    VH = 4 if even else 1
    NTP = 2 + KH
    with K.phase(f"att{layer}") as (sb, sem, block):
        q = sb("q", [P, U, QUAD])
        k = sb("k", [P, U, 2, KH * HD])
        v = sb("v", [P, U, 2, VH * HD])
        mask = sb("mask", [P, U, 2 * P], BF16)
        turned_sb = sb("turned_sb", [P, 2, NTP * P])
        probs = sb("probs", [P, 2, 4, 2 * P])
        probsT = sb("probsT", [P, 2, 8, P])
        outs = sb("outs", [P, U, OW])
        mx, negm = sb("mx", [P, 2, 4]), sb("negm", [P, 2, 4])
        den, rden, sink_e = sb("den", [P, 2, 4]), sb("rden", [P, 2, 4]), sb("sink_e", [P, 2, 4])
        sinks = sb("sinks", [P, 16])
        unit_in = [sem(f"unit_in{i}") for i in range(U)]
        turned, turned_out = Count(sem("turned")), Count(sem("turned_out"), 1)
        scored, lowered = Count(sem("scored"), 2), Count(sem("lowered"))
        exped, p_turned, p_out = Count(sem("exped"), 2), Count(sem("p_turned"), 2), [Count(sem("p_out0")), Count(sem("p_out1"), 1)]
        summed, o_out, stored = Count(sem("summed"), 4), Count(sem("o_out"), 1), Count(sem("stored"), U)
        st, own, sinks_in, sunk = sem("st"), sem("own"), sem("sinks_in"), Count(sem("sunk"))
        tp = ps[:, 0:NTP * P]
        op = ps[:, 3072:3072 + QUAD]
        sc = ps[:, 1024:3072].rearrange("p (b x y c) -> p b x y c", b=2, x=2, y=2)
        pp = ps[:, 3072:4096].rearrange("p (t c) -> p t c", c=P)

        def span(ap, dil, r, l0, c0, width):
            v_ = ap.rearrange("(l d) c -> d l c", d=dil)
            if not isinstance(r, int):
                return v_[bass.ds(r, 1), l0:l0 + P, c0:c0 + width].rearrange("d l c -> (d l) c")
            v_ = v_[r]
            return (v_[l0:l0 + P] if isinstance(l0, int) else v_[bass.ds(l0, P)])[:, c0:c0 + width]

        def walk(eng, visit):
            if even:
                visit(0, 0, 1, 0, 0, 0, True)
                for j in (1, 2, 3):
                    visit(j, j, 1, 0, j, 0, False)
                with eng.Fori(1, 4) as i:
                    for j in range(4):
                        visit(j, i * 4 + j, 1, 0, i * 4 + j, 0, False)
                for r in range(4):
                    visit(r, 16 + r, 4, r, 0, 1, True)
                with eng.Fori(1, 4) as b:
                    for r in range(4):
                        visit(r, b * 4 + (16 + r), 4, r, b, 1, False)
                with eng.Fori(0, 4) as i:
                    for j in range(4):
                        visit(j, i * 4 + (32 + j), 16, i * 4 + j, 0, 2, True)
            else:
                for j in range(4):
                    visit(j, j, 1, 0, 0, j, True)
                with eng.Fori(1, NT) as b:
                    for j in range(4):
                        visit(j, b * 4 + j, 1, 0, b, j, False)

        @block.sync
        def _(sp):
            if not even:
                sp.dma_start(sinks[:, :], K.x["sinks"].broadcast_to([P, 16])).then_inc(sinks_in, 16)
            if even:
                sp.dma_start(K.w_out0, K.x["w_out_even"].rearrange("a (p k) n -> p (a k) n", k=6)).then_inc(K.weights_in[1], 16)
                sp.dma_start(K.w_out1, K.x["w_out_odd"].rearrange("a (p k) n -> p (a k) n", k=DK)).then_inc(K.weights_in[3], 16)

            def load(j, n, dil, r, b, g, first):
                alone(sp, summed, n - 3, K.tick_sp)
                kc, vc = (g * QUAD, g * QUAD) if even else ((g // 2) * 2 * HD, (g // 2) * HD)
                kd, vd = (K.k_d, K.v_d) if even else (K.k1_d, K.v1_d)
                l0 = b * P
                before = l0 if first else l0 - P
                sp.dma_start(q[:, j, :], span(K.q_d, dil, r, l0, g * QUAD, QUAD)).then_inc(unit_in[j], 16)
                for half, at in enumerate((before, l0)):
                    sp.dma_start(k[:, j, half, :], span(kd, dil, r, at, kc, KH * HD)).then_inc(unit_in[j], 16)
                    sp.dma_start(v[:, j, half, :], span(vd, dil, r, at, vc, VH * HD)).then_inc(unit_in[j], 16)
                m = 2 if first else (0 if even else 1)
                sp.dma_start(mask[:, j, :], K.masks[:, m, :]).then_inc(unit_in[j], 16)
            walk(sp, load)

        @block.gpsimd
        def _(g_):
            g_.sem_inc(stored.sem, stored.credit)

            def store(j, n, dil, r, b, g, first):
                alone(g_, o_out, n + 1, K.tick)
                if even:
                    dst = span(K.o_d, dil, r, b * P, g * OW, OW)
                else:
                    dst = span(K.o1_d, dil, r, b * P, g * QUAD, QUAD)
                g_.dma_start(dst, outs[:, j, :]).then_inc(st, 16)
                g_.wait_ge(st, n * 16 + 16)
                g_.sem_inc(stored.sem, 1)
            walk(g_, store)

        @block.tensor
        def _(pe):
            for c in (scored, p_turned, summed):
                pe.sem_inc(c.sem, c.credit)

            def turn(s):
                j = s.slot(U)
                pe.wait_ge(unit_in[j], s.turn(U) * 96 + 96)
                until(pe, turned_out, s.n)
                for t in range(2):
                    nc.tensor.transpose(tp[:, t * P:(t + 1) * P], q[:, j, t * P:(t + 1) * P], K.ident[:, :])
                for pair in range(KH // 2):
                    for half in range(2):
                        at = (2 + 2 * pair + half) * P
                        last = nc.tensor.transpose(tp[:, at:at + P], k[:, j, half, pair * P:(pair + 1) * P], K.ident[:, :])
                last.then_inc(turned.sem, 1)

            def score(s):
                b = s.slot(2)
                until(pe, turned_out, s.n + 1)
                until(pe, exped, s.n - 1)
                qkT = turned_sb[:, b, :]
                for x in range(2):
                    nc.tensor.matmul(sc[:, b, x, :, :], K.identb[:, :],
                                     mask[:, s.slot(U), :].unsqueeze(1).broadcast_to([P, 2, 2 * P]), start=True, stop=False)
                for h in range(4):
                    lo = HD * (h % 2)
                    kp = h // 2 if even else 0
                    last = nc.tensor.matmul(sc[:, b, h % 2, h // 2, :], qkT[lo:lo + HD, (h // 2) * P:(h // 2 + 1) * P],
                                            qkT[lo:lo + HD, (2 + 2 * kp) * P:(4 + 2 * kp) * P], start=False, stop=(h >= 2))
                last.then_inc(scored.sem, 1)

            def turn_probs(s):
                until(pe, exped, s.n + 1)
                until(pe, o_out, s.n)
                until(pe, p_out[1], s.n)
                for h in range(4):
                    for half in range(2):
                        last = nc.tensor.transpose(pp[:, 2 * h + half, :], probs[:, s.slot(2), h, half * P:(half + 1) * P],
                                                   K.ident[:, :])
                last.then_inc(p_turned.sem, 1)

            def weigh(s):
                for h in range(4):
                    if h % 2 == 0:
                        until(pe, p_out[h // 2], s.n + 1)
                    vh = h if even else 0
                    for half in range(2):
                        last = nc.tensor.matmul(op[:, h * HD:(h + 1) * HD], probsT[:, s.slot(2), 2 * h + half, :],
                                                v[:, s.slot(U), half, vh * HD:(vh + 1) * HD],
                                                start=(half == 0), stop=(half == 1))
                last.then_inc(summed.sem, 1)

            def step(s):
                if s.plus(1).within(N):
                    score(s.plus(1))
                turn_probs(s)
                if s.plus(2).within(N):
                    turn(s.plus(2))
                weigh(s)
            s0 = Step(0, 0, U)
            turn(s0)
            score(s0)
            turn(s0.plus(1))
            looped(pe, N, U, U, step)

        @block.scalar
        def _(a):
            for c in (exped, turned_out, p_out[1]):
                a.sem_inc(c.sem, c.credit)

            def exps(s):
                b = s.slot(2)
                until(a, lowered, s.n + 1)
                until(a, p_turned, s.n - 1)
                if not even:
                    nc.scalar.activation(sink_e[:, b, :], sink_e[:, b, :], ACT.Exp).then_inc(sunk.sem, 1)
                for h in range(4):
                    total = outs[:, s.slot(U), QUAD + 4 + h:QUAD + 5 + h] if even else den[:, b, h:h + 1]
                    last = nc.scalar.activation(probs[:, b, h, :], sc[:, b, h % 2, h // 2, :], ACT.Exp, bias=negm[:, b, h:h + 1],
                                                scale=SCALE, accum_out=total)
                last.then_inc(exped.sem, 1)

            def turn_out(s):
                until(a, turned, s.n + 1)
                until(a, scored, s.n - 1)
                nc.scalar.activation(turned_sb[:, s.slot(2), :], tp, ACT.Copy).then_inc(turned_out.sem, 1)

            def step(s):
                until(a, p_turned, s.n + 1)
                until(a, summed, s.n - 1)
                nc.scalar.activation(probsT[:, s.slot(2), 4:8, :], pp[:, 4:8, :], ACT.Copy).then_inc(p_out[1].sem, 1)
                if s.plus(2).within(N):
                    turn_out(s.plus(2))
                if s.plus(1).within(N):
                    exps(s.plus(1))
            s0 = Step(0, 0, U)
            turn_out(s0)
            turn_out(s0.plus(1))
            exps(s0)
            looped(a, N, U, U, step)

        @block.vector
        def _(v_):
            own_ = Chain(v_, own)
            v_.sem_inc(o_out.sem, o_out.credit)
            if not even:
                v_.wait_ge(sinks_in, 16)

            def probs_out(s):
                until(v_, p_turned, s.n + 1)
                until(v_, summed, s.n - 1)
                nc.vector.tensor_copy(probsT[:, s.slot(2), 0:4, :], pp[:, 0:4, :]).then_inc(p_out[0].sem, 1)

            def lower(s):
                b = s.slot(2)
                until(v_, scored, s.n + 1)
                until(v_, stored, s.n - U + 1)
                own_.link(nc.vector.tensor_reduce(mx[:, b, :].rearrange("p (y x) -> p x y", y=2), sc[:, b, :, :, :], AX, ALU.max))
                if even:
                    own_.mark(nc.vector.tensor_scalar(outs[:, s.slot(U), QUAD:QUAD + 4], mx[:, b, :], SCALE, None, ALU.mult))
                    nc.vector.tensor_scalar(negm[:, b, :], mx[:, b, :], -SCALE, None, ALU.mult).then_inc(lowered.sem, 1)
                else:
                    u = s.slot(U)
                    own_.link(nc.vector.scalar_tensor_tensor(mx[:, b, :], mx[:, b, :], SCALE, sinks[:, 4 * u:4 * u + 4],
                                                             ALU.mult, ALU.max))
                    own_.mark(nc.vector.tensor_tensor(sink_e[:, b, :], sinks[:, 4 * u:4 * u + 4], mx[:, b, :], ALU.subtract))
                    nc.vector.tensor_scalar(negm[:, b, :], mx[:, b, :], -1.0, None, ALU.mult).then_inc(lowered.sem, 1)

            def out(s):
                b = s.slot(2)
                if even:
                    until(v_, summed, s.n + 1)
                    nc.vector.tensor_copy(outs[:, s.slot(U), 0:QUAD], op).then_inc(o_out.sem, 1)
                else:
                    until(v_, exped, s.n + 1)
                    own_.link(nc.vector.tensor_tensor(den[:, b, :], den[:, b, :], sink_e[:, b, :], ALU.add))
                    own_.link(nc.vector.reciprocal(rden[:, b, :], den[:, b, :]))
                    until(v_, summed, s.n + 1)
                    nc.vector.tensor_tensor(outs[:, s.slot(U), :].rearrange("p (h c) -> p h c", h=4),
                                            op.rearrange("p (h c) -> p h c", h=4),
                                            rden[:, b, :].unsqueeze(2).broadcast_to([P, 4, HD]), ALU.mult).then_inc(o_out.sem, 1)

            def step(s):
                if s.plus(1).within(N):
                    lower(s.plus(1))
                probs_out(s)
                out(s)
            lower(Step(0, 0, U))
            looped(v_, N, U, U, step, own_, 2 if even else 5)


def project_out(K, layer):
    nc, ps = K.nc, K.ps
    even = layer == 0
    NK = 6 if even else DK
    w = K.w_out0 if even else K.w_out1
    GW = QUAD + 8
    loads = 3 if even else 2
    with K.phase(f"out{layer}") as (sb, sem, block):
        ht = K.weights[:, 24 * D:26 * D].rearrange("p (b c) -> p b c", b=2)
        cat = sb("cat", [P, 2, NK * P])
        ot = sb("ot", [P, 2, 3, GW]) if even else None
        catT = sb("catT", [P, 2, NK, P])
        h2 = sb("h2", [P, 2, D])
        hn = sb("hn", [P, 2, D])
        hnT = sb("hnT", [P, DK, P])
        junk = sb("junk", [P, D], BF16)
        gain = sb("gain", [P, D])
        wr = sb("wr", [P, DK, NL])
        br = sb("br", [P, NL])
        lg = sb("lg", [P, 2, NL])
        ss, rs = sb("ss", [P, 2]), sb("rs", [P, 2])
        power = sb("power", [P, 1])
        if even:
            m, dm, wt, wd, ds = (sb(n, [P, s, 4]) for n, s in (("m", 1), ("dm", 3), ("wt", 3), ("wd", 3), ("ds", 1)))
            part = sb("part", [P, 3, QUAD])
        x_in = [sem("x_in0"), sem("x_in1")]
        par_in, own, pool_own, ready = sem("par_in"), sem("own"), sem("pool_own"), sem("ready")
        joined, diffed, weighed = Count(sem("joined")), Count(sem("diffed")), Count(sem("weighed"))
        c_turned, c_out = Count(sem("c_turned")), Count(sem("c_out"), 2)
        n_turned, n_out = Count(sem("n_turned")), Count(sem("n_out"))
        proj, added, sum_x, rms_x = Count(sem("proj")), Count(sem("added"), 2), Count(sem("sum_x"), 1), Count(sem("rms_x"))
        normed, routed, logged = Count(sem("normed")), Count(sem("routed")), Count(sem("logged"), 1)
        st, stored, st_lg, lg_stored = sem("st"), Count(sem("stored"), 2), sem("st_lg"), Count(sem("lg_stored"), 2)
        cp = ps[:, 0:NK * P]
        np_ = ps[:, 1024:2048]
        yp = ps[:, 2048:3072]
        rp = ps[:, 3072:3072 + NL]

        @block.sync
        def _(sp):
            sp.wait_ge(ready, 1)
            sp.dma_start(gain[:, :], K.x["norm_ffn"][layer:layer + 1].broadcast_to([P, D])).then_inc(par_in, 16)
            with nc.allow_non_contiguous_dma("router weights, 144 KB"):
                sp.dma_start(wr[:, :, 0:GROUPS], K.x["w_router_g"][layer].rearrange("(p k) g -> p k g", k=DK)).then_inc(par_in, 16)
                for g in range(GROUPS):
                    sp.dma_start(wr[:, :, GROUPS + g * EPG:GROUPS + (g + 1) * EPG],
                                 K.x["w_router_e"][layer, g].rearrange("(p k) e -> p k e", k=DK)).then_inc(par_in, 16)
            sp.dma_start(br[:, 0:GROUPS], K.x["b_router_g"][layer:layer + 1].broadcast_to([P, GROUPS])).then_inc(par_in, 16)
            sp.dma_start(br[:, GROUPS:NL], K.x["b_router_e"][layer:layer + 1].rearrange("a g e -> a (g e)").broadcast_to([P, NE])).then_inc(par_in, 16)

            def load(s):
                j, n = s.slot(2), s.n
                alone(sp, c_out, n - 1, K.tick_sp)
                alone(sp, added, n - 1, K.tick_sp)
                if even:
                    sp.dma_start(ht[:, j, :], rows(K.x["x"].rearrange("a t c -> (a t) c"), n)).then_inc(x_in[j], 16)
                    sp.dma_start(cat[:, j, 0:SGU], rows(K.a_d, n)).then_inc(x_in[j], 16)
                    sp.dma_start(ot[:, j, :, :].rearrange("p g c -> p (g c)"), rows(K.o_d, n)).then_inc(x_in[j], 16)
                else:
                    sp.dma_start(ht[:, j, :], rows(K.h_d[0][0:T], n)).then_inc(x_in[j], 16)
                    sp.dma_start(cat[:, j, :], rows(K.o1_d, n)).then_inc(x_in[j], 16)
            def step(s):
                n, j = s.n, s.slot(2)
                alone(sp, added, n + 1, K.tick_sp)
                sp.dma_start(rows(K.h_d[layer][0:T], n), h2[:, j, :]).then_inc(st, 16)
                if s.plus(2).within(NT):
                    load(s.plus(2))
                alone(sp, normed, n + 1, K.tick_sp)
                sp.dma_start(rows(K.hn_d[layer], n), hn[:, j, :]).then_inc(st, 16)
                sp.wait_ge(st, n * 32 + 32)
                sp.sem_inc(stored.sem, 1)
                if not isinstance(n, int) or n >= 2:
                    store_lg(s.plus(-2))

            def store_lg(s):
                alone(sp, logged, s.n + 1, K.tick_sp)
                sp.dma_start(rows(K.lg_d[layer], s.n), lg[:, s.slot(2), :]).then_inc(st_lg, 16)
                sp.wait_ge(st_lg, s.n * 16 + 16)
                sp.sem_inc(lg_stored.sem, 1)
            for c in (stored, lg_stored):
                sp.sem_inc(c.sem, c.credit)
            s0 = Step(0, 0, 2)
            load(s0)
            load(s0.plus(1))
            step(s0)
            for e in range(2):
                load_expert(K, sp, layer, e, e)
            step(s0.plus(1))
            with sp.Fori(1, NT // 2 - 1) as i:
                for j in range(2):
                    step(Step(i, j, 2))
            end = Step(NT // 2 - 1, 0, 2)
            step(end)
            step(end.plus(1))
            store_lg(end)
            store_lg(end.plus(1))
            if even:
                sp.dma_start(K.w_in1, K.x["w_in_odd"].rearrange("a (p k) n -> p (a k) n", k=DK)).then_inc(K.weights_in[2], 16)

        @block.tensor
        def _(pe):

            def turn_cat(s):
                j = s.slot(2)
                if even:
                    until(pe, joined, s.n + 1)
                else:
                    pe.wait_ge(x_in[j], s.turn(2) * 32 + 32)
                until(pe, c_out, s.n)
                src = cat[:, j, :].rearrange("p (c k) -> p k c", k=NK)
                for k in range(NK):
                    last = nc.tensor.transpose(cp[:, k * P:(k + 1) * P], src[:, k, :], K.ident[:, :])
                last.then_inc(c_turned.sem, 1)

            def turn_hn(s):
                until(pe, normed, s.n + 1)
                src = hn[:, s.slot(2), :].rearrange("p (c k) -> p k c", k=DK)
                for k in range(DK):
                    last = nc.tensor.transpose(np_[:, k * P:(k + 1) * P], src[:, k, :], K.ident[:, :])
                last.then_inc(n_turned.sem, 1)

            def project(s):
                until(pe, c_out, s.n + 1)
                until(pe, added, s.n)
                for half in range(2):
                    for k in range(NK):
                        last = nc.tensor.matmul(yp[:, 512 * half:512 * (half + 1)], catT[:, s.slot(2), k, :],
                                                w[:, k, 512 * half:512 * (half + 1)], start=(k == 0), stop=(k == NK - 1))
                last.then_inc(proj.sem, 1)

            def router(s):
                until(pe, n_out, s.n + 1)
                until(pe, logged, s.n)
                for k in range(DK):
                    last = nc.tensor.matmul(rp, hnT[:, k, :], wr[:, k, :], start=(k == 0), stop=(k == DK - 1))
                last.then_inc(routed.sem, 1)

            def step(s):
                project(s)
                if s.plus(1).within(NT):
                    turn_cat(s.plus(1))
                if not isinstance(s.n, int) or s.n >= 2:
                    router(s.plus(-2))
                if not isinstance(s.n, int) or s.n >= 1:
                    turn_hn(s.plus(-1))
            s0 = Step(0, 0, 2)
            turn_cat(s0)
            pe.wait_ge(K.weights_in[1 if even else 3], 16)
            pe.wait_ge(par_in, 16 * 8)
            step(s0)
            step(s0.plus(1))
            with pe.Fori(1, NT // 2 - 1) as i:
                for j in range(2):
                    step(Step(i, j, 2))
            end = Step(NT // 2 - 1, 0, 2)
            step(end)
            step(end.plus(1))
            router(end)
            turn_hn(end.plus(1))
            router(end.plus(1))

        @block.scalar
        def _(a):
            if even:
                def weights(s):
                    until(a, diffed, s.n + 1)
                    nc.scalar.activation(wt[:, :, :], dm[:, :, :], ACT.Exp).then_inc(weighed.sem, 1)
                weights(Step(0, 0, 2))

            a.sem_inc(sum_x.sem, sum_x.credit)

            def step(s):
                if even and s.plus(1).within(NT):
                    weights(s.plus(1))
                until(a, added, s.n + 1)
                until(a, sum_x, s.n)
                nc.scalar.activation(junk[:, :], h2[:, s.slot(2), :], ACT.Square, accum_out=ss[:, s.slot(2):s.slot(2) + 1]).then_inc(sum_x.sem, 1)
            looped(a, NT, 2, 2, step)

        @block.gpsimd
        def _(g):
            own_ = Chain(g, pool_own)
            own_.link(g.memset(power[:, :], -0.5))

            def step(s):
                j = s.slot(2)
                alone(g, sum_x, s.n + 1, K.tick)
                own_.link(g.tensor_scalar(rs[:, j:j + 1], ss[:, j:j + 1], 1.0 / D, EPS, ALU.mult, ALU.add))
                g.tensor_tensor(rs[:, j:j + 1], rs[:, j:j + 1], power[:, 0:1], ALU.pow).then_inc(rms_x.sem, 1)
            looped(g, NT, 2, 0, step, own_, 1)

        @block.vector
        def _(v_):
            own_ = Chain(v_, own)
            for c in (c_out, added, logged):
                v_.sem_inc(c.sem, c.credit)
            v_.sem_inc(ready, 1)

            def join(s):
                j = s.slot(2)
                v_.wait_ge(x_in[j], s.turn(2) * (16 * loads) + 16 * loads)
                if not even:
                    return
                mm, dd = ot[:, j, :, QUAD:QUAD + 4], ot[:, j, :, QUAD + 4:QUAD + 8]
                own_.link(nc.vector.tensor_tensor(m[:, 0, :], mm[:, 0, :], mm[:, 1, :], ALU.max))
                own_.link(nc.vector.tensor_tensor(m[:, 0, :], m[:, 0, :], mm[:, 2, :], ALU.max))
                nc.vector.tensor_tensor(dm[:, :, :], mm, m[:, :, :].broadcast_to([P, 3, 4]), ALU.subtract).then_inc(diffed.sem, 1)
                until(v_, weighed, s.n + 1)
                own_.link(nc.vector.tensor_tensor(wd[:, :, :], wt[:, :, :], dd, ALU.mult))
                own_.link(nc.vector.tensor_tensor(ds[:, 0, :], wd[:, 0, :], wd[:, 1, :], ALU.add))
                own_.link(nc.vector.tensor_tensor(ds[:, 0, :], ds[:, 0, :], wd[:, 2, :], ALU.add))
                own_.link(nc.vector.reciprocal(ds[:, 0, :], ds[:, 0, :]))
                own_.link(nc.vector.tensor_tensor(wd[:, :, :], wt[:, :, :], ds[:, :, :].broadcast_to([P, 3, 4]), ALU.mult))
                for g in range(3):
                    own_.mark(nc.vector.tensor_tensor(part[:, g, :].rearrange("p (h c) -> p h c", h=4),
                                                      ot[:, j, g, 0:QUAD].rearrange("p (h c) -> p h c", h=4),
                                                      wd[:, g, :].unsqueeze(2).broadcast_to([P, 4, HD]), ALU.mult))
                own_.meet()
                own_.link(nc.vector.tensor_tensor(part[:, 0, :], part[:, 0, :], part[:, 1, :], ALU.add))
                nc.vector.tensor_tensor(cat[:, j, SGU:SGU + QUAD], part[:, 0, :], part[:, 2, :], ALU.add).then_inc(joined.sem, 1)

            def cat_out(s):
                until(v_, c_turned, s.n + 1)
                nc.vector.tensor_copy(catT[:, s.slot(2), :, :], cp.rearrange("p (k c) -> p k c", k=NK)).then_inc(c_out.sem, 1)

            def hn_out(s):
                until(v_, n_turned, s.n + 1)
                nc.vector.tensor_copy(hnT[:, :, :], np_.rearrange("p (k c) -> p k c", k=DK)).then_inc(n_out.sem, 1)

            def add(s):
                j = s.slot(2)
                until(v_, proj, s.n + 1)
                until(v_, stored, s.n - 1)
                nc.vector.tensor_tensor(h2[:, j, :], yp, ht[:, j, :], ALU.add).then_inc(added.sem, 1)

            def norm(s):
                j = s.slot(2)
                until(v_, rms_x, s.n + 1)
                nc.vector.scalar_tensor_tensor(hn[:, j, :], h2[:, j, :], rs[:, j:j + 1], gain[:, :], ALU.mult, ALU.mult).then_inc(normed.sem, 1)

            def log(s):
                j = s.slot(2)
                until(v_, routed, s.n + 1)
                until(v_, lg_stored, s.n - 1)
                nc.vector.tensor_tensor(lg[:, j, :], rp, br[:, :], ALU.add).then_inc(logged.sem, 1)

            def step(s):
                if not isinstance(s.n, int) or s.n >= 1:
                    norm(s.plus(-1))
                if s.plus(1).within(NT):
                    join(s.plus(1))
                add(s)
                if s.plus(1).within(NT):
                    cat_out(s.plus(1))
                if not isinstance(s.n, int) or s.n >= 2:
                    log(s.plus(-2))
                if not isinstance(s.n, int) or s.n >= 1:
                    hn_out(s.plus(-1))
            s0 = Step(0, 0, 2)
            join(s0)
            cat_out(s0)
            v_.wait_ge(par_in, 16 * 8)
            step(s0)
            step(s0.plus(1))
            per, start = (11 if even else 0), own_.n
            with v_.Fori(1, NT // 2 - 1) as i:
                own_.base, own_.n = (i - 1) * (2 * per) + start, 0
                for j in range(2):
                    step(Step(i, j, 2))
                assert own_.n == 2 * per, own_.n / 2
            own_.base, own_.n = start + (NT // 2 - 2) * 2 * per, 0
            end = Step(NT // 2 - 1, 0, 2)
            step(end)
            step(end.plus(1))
            log(end)
            norm(end.plus(1))
            hn_out(end.plus(1))
            log(end.plus(1))


def load_expert(K, sp, layer, e, slot):
    nc = K.nc
    for n, name in enumerate(("w_gate", "w_up")):
        src = K.x[name][layer].rearrange("e (p k) f -> e p (k f)", k=DK)
        src = src[e] if isinstance(e, int) else src[bass.ds(e, 1)].rearrange("a p f -> (a p) f")
        dst = K.expert_w[:, slot, n * DK * FF:(n + 1) * DK * FF]
        sp.dma_start(dst, src).then_inc(K.expert_in[layer][slot], 16)
    src = K.x["w_down"][layer].rearrange("e (p k) n -> e p (k n)", k=2)
    src = src[e] if isinstance(e, int) else src[bass.ds(e, 1)].rearrange("a p n -> (a p) n")
    sp.dma_start(K.expert_w[:, slot, DK * 2 * FF:], src).then_inc(K.expert_in[layer][slot], 16)


def route(K, layer):
    nc, ps = K.nc, K.ps
    with K.phase(f"route{layer}") as (sb, sem, block):
        lg = sb("lg", [P, NT, NL])
        iota4, iota32 = sb("iota4", [P, GROUPS]), sb("iota32", [P, NE])
        iota_i = sb("iota_i", [P, NE], I32)
        gm, gi, gs = sb("gm", [P, NT]), sb("gi", [P, NT]), sb("gs", [P, NT])
        gx, gone = sb("gx", [P, NT, GROUPS]), sb("gone", [P, NT, GROUPS])
        le, cand = sb("le", [P, NT, NE]), sb("cand", [P, NT, NE])
        one = sb("one", [P, 2, NT, NE])
        both = sb("both", [P, NT, NE], BF16)
        best = sb("best", [P, 2, NT])
        rank, base = sb("rank", [P, NT, NE]), sb("base", [P, NT, NE])
        e2, gate = sb("e2", [P, NT]), sb("gate", [P, 2, NT])
        count, blocks, ends, zero = (sb(n, [P, NE]) for n in ("count", "blocks", "ends", "zero"))
        count_i = sb("count_i", [P, NE], I32)
        place, place_i, low_i, high_i = sb("place", [P, 2, NT]), *(sb(n, [P, 2, NT], I32) for n in ("place_i", "low_i", "high_i"))
        low, high = sb("low", [P, 2, NT]), sb("high", [P, 2, NT])
        token = sb("token", [P, NT], I32)
        token_f = sb("token_f", [P, NT])
        iota_p, iota_row = sb("iota_p", [P, P], I32), sb("iota_row", [P, P])
        spare_i, spare = sb("spare_i", [P, 1], I32), sb("spare", [P, 1])
        at_row = K.weights[:, 0:2 * NT * P].rearrange("p (n c) -> p n c", c=P)
        at_block = sb("at_block", [P, 2 * NT, 3, NBMAX])
        found = sb("found", [P, 3, NBMAX])
        in_, own, pool_own, exp_in, exp_out = (sem(n) for n in ("in", "own", "pool_own", "exp_in", "exp_out"))
        made, both_done, counted, placed, gathered = (sem(n) for n in
            ("made", "both_done", "counted", "placed", "gathered"))
        table = ps[:, 1024:1024 + 3 * NBMAX].rearrange("p (f b) -> p f b", f=3)
        wide4, wide32 = [P, NT, GROUPS], [P, NT, NE]
        pre = ps[:, 0:NT * NE].rearrange("p (n e) -> p n e", n=NT)
        tot = ps[:, 512:512 + NT * NE].rearrange("p (n e) -> p n e", n=NT)

        @block.sync
        def _(sp):
            sp.dma_start(lg[:, :, :], K.lg_d[layer].rearrange("(n p) c -> p n c", p=P)).then_inc(in_, 16)

        @block.gpsimd
        def _(g):
            g.iota(iota_i[:, :], pattern=[[1, NE]], base=0, channel_multiplier=0).then_inc(made, 1)
            g.iota(token[:, :], pattern=[[P, NT]], base=0, channel_multiplier=1).then_inc(made, 1)
            g.iota(iota_p[:, :], pattern=[[1, P]], base=0, channel_multiplier=0).then_inc(made, 1)
            g.iota(spare_i[:, :], pattern=[[0, 1]], base=T, channel_multiplier=1).then_inc(made, 1)

        @block.scalar
        def _(a):
            a.wait_ge(exp_in, 1)
            nc.scalar.activation(gx[:, :, :], gx[:, :, :], ACT.Exp).then_inc(exp_out, 1)
            a.wait_ge(exp_in, 2)
            nc.scalar.activation(e2[:, :], e2[:, :], ACT.Exp).then_inc(exp_out, 1)

        @block.tensor
        def _(pe):
            pe.wait_ge(both_done, 1)
            flat = both[:, :, :].rearrange("p n e -> p (n e)")
            nc.tensor.matmul(ps[:, 0:NT * NE], K.before[:, :], flat, start=True, stop=True)
            nc.tensor.matmul(ps[:, 512:512 + NT * NE], K.onesb[:, :], flat, start=True, stop=True).then_inc(counted, 1)
            pe.wait_ge(placed, 1)
            for n in range(2 * NT):
                last = nc.tensor.matmul(table, at_row[:, n, :], at_block[:, n, :, :], start=(n == 0), stop=(n == 2 * NT - 1))
            last.then_inc(gathered, 1)

        @block.vector
        def _(v):
            V = nc.vector
            own_ = Chain(v, own)
            do = own_.link
            v.wait_ge(made, 4)
            do(V.tensor_copy(iota32[:, :], iota_i[:, :]))
            do(V.tensor_copy(iota4[:, :], iota_i[:, 0:GROUPS]))
            do(V.tensor_copy(token_f[:, :], token[:, :]))
            do(V.memset(zero[:, :], 0.0))
            do(V.tensor_copy(iota_row[:, :], iota_p[:, :]))
            do(V.tensor_copy(spare[:, :], spare_i[:, :]))
            v.wait_ge(in_, 16)
            lgg = lg[:, :, 0:GROUPS]
            i4 = iota4[:, :].unsqueeze(1).broadcast_to(wide4)
            i32 = iota32[:, :].unsqueeze(1).broadcast_to(wide32)

            def bc(t, wide):
                return t.unsqueeze(2).broadcast_to(wide)

            do(V.tensor_reduce(gm[:, :], lgg, AX, ALU.max))
            do(V.tensor_tensor(gx[:, :, :], lgg, bc(gm[:, :], wide4), ALU.is_lt))
            do(V.scalar_tensor_tensor(gx[:, :, :], gx[:, :, :], BIG, i4, ALU.mult, ALU.add))
            do(V.tensor_reduce(gi[:, :], gx[:, :, :], AX, ALU.min))
            do(V.tensor_tensor(gone[:, :, :], i4, bc(gi[:, :], wide4), ALU.is_equal))
            V.tensor_tensor(gx[:, :, :], lgg, bc(gm[:, :], wide4), ALU.subtract).then_inc(exp_in, 1)
            leg = le[:, :, :].rearrange("p n (g e) -> p (n g) e", g=GROUPS)
            go = gone[:, :, :].rearrange("p n g -> p (n g)").unsqueeze(2).broadcast_to([P, NT * GROUPS, EPG])
            do(V.tensor_copy(le[:, :, :], lg[:, :, GROUPS:NL]))
            do(V.tensor_tensor(leg, leg, go, ALU.mult))
            do(V.tensor_scalar(gone[:, :, :], gone[:, :, :], -NEG, NEG, ALU.mult, ALU.add))
            do(V.tensor_tensor(leg, leg, go, ALU.add))
            for k in range(2):
                do(V.tensor_reduce(best[:, k, :], le[:, :, :], AX, ALU.max))
                do(V.tensor_tensor(cand[:, :, :], le[:, :, :], bc(best[:, k, :], wide32), ALU.is_lt))
                do(V.scalar_tensor_tensor(cand[:, :, :], cand[:, :, :], BIG, i32, ALU.mult, ALU.add))
                do(V.tensor_reduce(gi[:, :], cand[:, :, :], AX, ALU.min))
                do(V.tensor_tensor(one[:, k, :, :], i32, bc(gi[:, :], wide32), ALU.is_equal))
                if k == 0:
                    do(V.scalar_tensor_tensor(le[:, :, :], one[:, 0, :, :], 2 * NEG, le[:, :, :], ALU.mult, ALU.add))
            V.tensor_tensor(both[:, :, :], one[:, 0, :, :], one[:, 1, :, :], ALU.add).then_inc(both_done, 1)
            V.tensor_tensor(e2[:, :], best[:, 1, :], best[:, 0, :], ALU.subtract).then_inc(exp_in, 1)
            v.wait_ge(exp_out, 2)
            do(V.tensor_reduce(gs[:, :], gx[:, :, :], AX, ALU.add))
            do(V.tensor_scalar(best[:, 0, :], e2[:, :], 1.0, None, ALU.add))
            do(V.tensor_tensor(gs[:, :], gs[:, :], best[:, 0, :], ALU.mult))
            do(V.reciprocal(gate[:, 0, :], gs[:, :]))
            do(V.tensor_tensor(gate[:, 1, :], gate[:, 0, :], e2[:, :], ALU.mult))
            v.wait_ge(counted, 1)
            do(V.memset(base[:, 0, :], 0.0))
            for n in range(1, NT):
                do(V.tensor_tensor(base[:, n, :], base[:, n - 1, :], tot[:, n - 1, :], ALU.add))
            do(V.tensor_tensor(count[:, :], base[:, NT - 1, :], tot[:, NT - 1, :], ALU.add))
            do(V.tensor_tensor(rank[:, :, :], base[:, :, :], pre, ALU.add))
            do(V.tensor_scalar(count_i[:, :], count[:, :], float(P - 1), None, ALU.add))
            do(V.tensor_scalar(count_i[:, :], count_i[:, :], 7, None, ALU.arith_shift_right))
            do(V.tensor_scalar(blocks[:, :], count_i[:, :], 1.0, None, ALU.max))
            do(V.tensor_tensor_scan(ends[:, :], blocks[:, :], zero[:, :], 0.0, ALU.add, ALU.add))
            do(V.memset(K.ends_i[:, 0:1], 0))
            do(V.tensor_copy(K.ends_i[:, 1:NE + 1], ends[0:1, :]))
            do(V.tensor_tensor(ends[:, :], ends[:, :], blocks[:, :], ALU.subtract))
            do(V.scalar_tensor_tensor(rank[:, :, :], ends[:, :].unsqueeze(1).broadcast_to(wide32), float(P), rank[:, :, :],
                                      ALU.mult, ALU.add))
            for k in range(2):
                do(V.tensor_tensor(one[:, k, :, :], one[:, k, :, :], rank[:, :, :], ALU.mult))
                do(V.tensor_reduce(place[:, k, :], one[:, k, :, :], AX, ALU.add))
            do(V.tensor_copy(place_i[:, :, :], place[:, :, :]))
            do(V.tensor_scalar(low_i[:, :, :], place_i[:, :, :], P - 1, None, ALU.bitwise_and))
            do(V.tensor_scalar(high_i[:, :, :], place_i[:, :, :], 7, None, ALU.arith_shift_right))
            do(V.tensor_copy(low[:, :, :], low_i[:, :, :]))
            do(V.tensor_copy(high[:, :, :], high_i[:, :, :]))
            lows, highs, gates = (t[:, :, :].rearrange("p k n -> p (k n)") for t in (low, high, gate))
            rows_, blocks_ = [P, 2 * NT, P], [P, 2 * NT, NBMAX]
            own_.mark(V.tensor_tensor(at_row[:, :, :], iota_row[:, :].unsqueeze(1).broadcast_to(rows_),
                                      lows.unsqueeze(2).broadcast_to(rows_), ALU.is_equal))
            do(V.tensor_tensor(at_block[:, :, 0, :], iota_row[:, 0:NBMAX].unsqueeze(1).broadcast_to(blocks_),
                               highs.unsqueeze(2).broadcast_to(blocks_), ALU.is_equal))
            for k in range(2):
                at = slice(k * NT, (k + 1) * NT)
                own_.mark(V.tensor_tensor(at_block[:, at, 1, :], at_block[:, at, 0, :],
                                          token_f[:, :].unsqueeze(2).broadcast_to([P, NT, NBMAX]), ALU.mult))
            do(V.tensor_tensor(at_block[:, :, 2, :], at_block[:, :, 0, :], gates.unsqueeze(2).broadcast_to(blocks_), ALU.mult))
            v.sem_inc(placed, 1)
            v.wait_ge(gathered, 1)
            do(V.tensor_copy(found[:, :, :], table))
            own_.mark(V.tensor_copy(K.who[:, :], found[:, 1, :]))
            own_.mark(V.tensor_copy(K.gates[:, :], found[:, 2, :]))
            do(V.tensor_scalar(found[:, 0, :], found[:, 0, :], -1.0, 1.0, ALU.mult, ALU.add))
            do(V.scalar_tensor_tensor(K.where[:, :], found[:, 0, :], spare[:, 0:1], found[:, 1, :], ALU.mult, ALU.add))


def experts(K, layer):
    nc, ps = K.nc, K.ps
    with K.phase(f"moe{layer}") as (sb, sem, block):
        xg = sb("xg", [P, D])
        xT = sb("xT", [P, DK, P])
        silu, hid = sb("silu", [P, FF]), sb("hid", [P, FF])
        hidT = sb("hidT", [P, 2, P])
        y = sb("y", [P, D])
        who, where = sb("who", [P, 1], I32), sb("where", [P, 1], I32)
        gate = sb("gate", [P, 1])
        gathered_s, scattered_s = sem("gathered"), sem("scattered")
        who_set, where_set = Count(sem("who_set")), Count(sem("where_set"))
        x_turned, x_out = Count(sem("x_turned")), Count(sem("x_out"))
        up, act_done, hid_done = Count(sem("up")), Count(sem("act_done")), Count(sem("hid_done"))
        h_turned, h_out, down = Count(sem("h_turned")), Count(sem("h_out")), Count(sem("down"))
        y_out, gated = Count(sem("y_out"), 1), Count(sem("gated"))
        gup = ps[:, 0:2 * FF]
        xp = ps[:, 512:512 + D]
        hp = ps[:, 1536:1536 + 2 * P]
        yp = ps[:, 2048:2048 + D]
        lim = dict(min_val=1, max_val=64)

        def end_of(eng, at):
            src = K.ends_i[0:1, at:at + 1] if isinstance(at, int) else K.ends_i[0:1, bass.ds(at, 1)]
            return eng.value_load(src, **lim)

        @block.sync
        def _(sp):
            with sp.Fori(1, NE // 2) as i:
                for j in range(2):
                    alone(sp, down, end_of(sp, i * 2 + (j - 1)), K.tick_sp)
                    load_expert(K, sp, layer, i * 2 + j, j)

        @block.gpsimd
        def _(g):
            def gather(m):
                nc.gpsimd.tensor_copy(who[:, :], K.who[:, m:m + 1] if isinstance(m, int) else K.who[:, bass.ds(m, 1)]).then_inc(who_set.sem, 1)
                alone(g, who_set, m + 1, K.tick)
                nc.gpsimd.indirect_dma_start(xg[:, :], None, K.hn_d[layer],
                                             bass.IndirectOffsetOnAxis(ap=who[:, :], axis=0)).then_inc(gathered_s, 16)
            gather(0)
            g.dma_start(where[:, :], K.where[:, 0:1]).then_inc(scattered_s, 16)
            g.wait_ge(gathered_s, 16)
            until(g, x_turned, 1)
            gather(1)
            total = end_of(g, NE)
            with g.Fori(0, total) as m:
                nc.gpsimd.tensor_copy(gate[:, :], K.gates[:, bass.ds(m, 1)]).then_inc(gated.sem, 1)
                alone(g, x_turned, m + 2, K.tick)
                gather(m + 2)
                g.wait_ge(scattered_s, m * 16 + 16)
                g.sem_inc(K.tick, 1)
                nc.gpsimd.tensor_copy(where[:, :], K.where[:, bass.ds(m, 1)]).then_inc(where_set.sem, 1)
                alone(g, where_set, m + 1, K.tick)
                alone(g, y_out, m + 1, K.tick)
                nc.gpsimd.indirect_dma_start(K.h_d[layer], bass.IndirectOffsetOnAxis(ap=where[:, :], axis=0), y[:, :], None,
                                             compute_op=ALU.add).then_inc(scattered_s, 16)
            g.wait_ge(gathered_s, total * 16 + 32)
            g.sem_inc(K.tick, 1)
            g.wait_ge(scattered_s, total * 16 + 16)
            g.sem_inc(K.tick, 1)

        @block.tensor
        def _(pe):
            def turn_x(m):
                pe.wait_ge(gathered_s, m * 16 + 16)
                src = xg[:, :].rearrange("p (c k) -> p k c", k=DK)
                for k in range(DK):
                    last = nc.tensor.transpose(xp[:, k * P:(k + 1) * P], src[:, k, :], K.ident[:, :])
                last.then_inc(x_turned.sem, 1)

            turn_x(0)
            with pe.Fori(0, NE // 2) as i:
                for j in range(2):
                    wgu = K.expert_w[:, j, 0:DK * 2 * FF].rearrange("p (s k f) -> p k s f", s=2, k=DK)
                    wd = K.expert_w[:, j, DK * 2 * FF:].rearrange("p (k n) -> p k n", k=2)
                    pe.wait_ge(K.expert_in[layer][j], i * 48 + 48)
                    pe.sem_inc(K.tick_pe, 1)
                    first = pe.value_load(K.ends_i[0:1, bass.ds(i * 2 + j, 1)], min_val=0, max_val=64)
                    with pe.Fori(first, end_of(pe, i * 2 + (j + 1))) as m:
                        until(pe, x_out, m + 1)
                        for k in range(DK):
                            last = nc.tensor.matmul(gup, xT[:, k, :], wgu[:, k, :, :], start=(k == 0), stop=(k == DK - 1))
                        last.then_inc(up.sem, 1)
                        turn_x(m + 1)
                        until(pe, hid_done, m + 1)
                        src = hid[:, :].rearrange("p (c k) -> p k c", k=2)
                        for k in range(2):
                            last = nc.tensor.transpose(hp[:, k * P:(k + 1) * P], src[:, k, :], K.ident[:, :])
                        last.then_inc(h_turned.sem, 1)
                        until(pe, h_out, m + 1)
                        until(pe, y_out, m)
                        for half in range(2):
                            for k in range(2):
                                last = nc.tensor.matmul(yp[:, 512 * half:512 * (half + 1)], hidT[:, k, :],
                                                        wd[:, k, 512 * half:512 * (half + 1)], start=(k == 0), stop=(k == 1))
                        last.then_inc(down.sem, 1)

        @block.scalar
        def _(a):
            a.sem_inc(y_out.sem, y_out.credit)
            with a.Fori(0, end_of(a, NE)) as m:
                until(a, up, m + 1)
                nc.scalar.activation(silu[:, :], gup[:, 0:FF], ACT.Silu).then_inc(act_done.sem, 1)
                until(a, down, m + 1)
                until(a, gated, m + 1)
                a.wait_ge(scattered_s, m * 16 + 16)
                nc.scalar.activation(y[:, :], yp, ACT.Copy, scale=gate[:, 0:1]).then_inc(y_out.sem, 1)

        @block.vector
        def _(v):
            def turn_out(m):
                until(v, x_turned, m + 1)
                nc.vector.tensor_copy(xT[:, :, :], xp.rearrange("p (k c) -> p k c", k=DK)).then_inc(x_out.sem, 1)
            turn_out(0)
            with v.Fori(0, end_of(v, NE)) as m:
                until(v, act_done, m + 1)
                nc.vector.tensor_tensor(hid[:, :], silu[:, :], gup[:, FF:2 * FF], ALU.mult).then_inc(hid_done.sem, 1)
                until(v, h_turned, m + 1)
                nc.vector.tensor_copy(hidT[:, :, :], hp.rearrange("p (k c) -> p k c", k=2)).then_inc(h_out.sem, 1)
                turn_out(m + 1)


NAMES = ["x", "positions", "norm_mix", "norm_ffn", "w_in_even", "w_out_even", "sgu_norm", "sgu_w", "sgu_b",
         "qn_dil", "kn_dil", "w_in_odd", "w_out_odd", "qn_swa", "kn_swa", "sinks", "w_router_g", "b_router_g",
         "w_router_e", "b_router_e", "w_gate", "w_up", "w_down"]


def kernel(**inputs):
    import concourse.bacc as bacc
    from concourse.bass_utils import run_bass_kernel_spmd

    nc = bacc.Bacc("TRN2", target_bir_lowering=False, num_devices=1)
    arrays, ins = {}, {}
    for name in NAMES:
        a = np.ascontiguousarray(inputs[name])
        arrays[f"in_{name}"] = a
        ins[name] = nc.dram_tensor(f"in_{name}", a.shape, mybir.dt.from_np(a.dtype), kind="ExternalInput").ap()
    out = nc.dram_tensor("out", (T + P, D), F32, kind="ExternalOutput").ap()
    Kernel(nc, ins, out).build()
    r = run_bass_kernel_spmd(nc, [arrays], core_ids=[0])
    return r.results[0]["out"][0:T].reshape(1, T, D)
```

```python
import concourse.bass as bass
from concourse import mybir
from contextlib import ExitStack, contextmanager
import numpy as np

F32 = mybir.dt.float32
F32R = mybir.dt.float32r
BF16 = mybir.dt.bfloat16
I32 = mybir.dt.int32
ACT = mybir.ActivationFunctionType
ALU = mybir.AluOpType
AX = mybir.AxisListType.X

P = 128
T = 2048
D = 1024
DK = D // P
NT = T // P
HD = 64
ROT = HD // 4
HALF = ROT // 2
THETA = 500000.0
EPS = 1e-6
SCALE = HD ** -0.5
SGU = 512
SG = 8
DIL = ((1, 16), (4, 4), (16, 1))
NDH = 12
DW = NDH * HD
QUAD = 4 * HD
GROUPS, EPG = 4, 8
NE = GROUPS * EPG
FF = 256
NL = GROUPS + NE
NBMAX = 68
NEG = -1e30
BIG = 1e6


class Count:

    def __init__(self, sem, credit=0):
        self.sem, self.credit = sem, credit


class Step:

    def __init__(self, i, j, u):
        self.i, self.j, self.u = i, j, u
        self.n = i * u + j

    def within(self, total):
        return not isinstance(self.n, int) or self.n < total

    def plus(self, k):
        q, j = divmod(self.j + k, self.u)
        return Step(self.i + q, j, self.u)

    def slot(self, m):
        return self.j % m

    def turn(self, m):
        return self.i * (self.u // m) + self.j // m


def until(eng, count, k):
    eng.wait_ge(count.sem, k + count.credit)


def alone(eng, count, k, tick):
    eng.wait_ge(count.sem, k + count.credit)
    eng.sem_inc(tick, 1)


class Chain:

    def __init__(self, eng, sem, tick=None):
        self.eng, self.sem, self.tick = eng, sem, tick
        self.base, self.n = 0, 0

    def link(self, ins):
        ins.then_inc(self.sem, 1)
        self.n += 1
        self.eng.wait_ge(self.sem, self.base + self.n)
        if self.tick is not None:
            self.eng.sem_inc(self.tick, 1)

    def mark(self, ins):
        ins.then_inc(self.sem, 1)
        self.n += 1

    def meet(self):
        self.eng.wait_ge(self.sem, self.base + self.n)
        if self.tick is not None:
            self.eng.sem_inc(self.tick, 1)


def looped(eng, total, u, tail, step, chain=None, per=0, head=0):
    rounds = (total - tail) // u
    for n in range(head * u):
        step(Step(n // u, n % u, u))
    start = chain.base + chain.n if chain else 0
    with eng.Fori(head, rounds) as i:
        if chain:
            chain.base, chain.n = (i - head if head else i) * (per * u) + start, 0
        for j in range(u):
            step(Step(i, j, u))
        if chain:
            assert chain.n == per * u, f"the chain has {chain.n / u} links a step"
    if chain:
        chain.base, chain.n = start + (rounds - head) * per * u, 0
    for n in range(rounds * u, total):
        step(Step(n // u, n % u, u))


def rows(ap, n):
    v = ap.rearrange("(n p) c -> n p c", p=P)
    if isinstance(n, int):
        return v[n]
    return v[bass.ds(n, 1)].rearrange("a p c -> (a p) c")


class Kernel:
    def __init__(self, nc, ins, out):
        self.nc, self.x, self.out = nc, ins, out
        self.ctx = ExitStack()

    def dram(self, name, shape, dt=F32):
        return self.nc.dram_tensor(name, shape, dt).ap()

    @contextmanager
    def phase(self, name):
        sems = []
        with ExitStack() as s:
            def sb(n, shape, dt=F32):
                return s.enter_context(self.nc.sbuf_tensor(f"{name}_{n}", shape, dt))

            def sem(n):
                sems.append(self.nc.alloc_semaphore(name=f"{name}_{n}"))
                return sems[-1]

            yield sb, sem, s.enter_context(self.nc.Block())
        self.nc.clear_and_free_semaphores(sems)
        self.nc.all_engine_barrier()

    def build(self):
        nc = self.nc
        with self.ctx:
            keep = lambda n, shape, dt=F32: self.ctx.enter_context(nc.sbuf_tensor(n, shape, dt))
            self.ident = keep("ident", [P, P])
            self.identb = keep("identb", [P, P], BF16)
            self.masks = keep("masks", [P, 3, 2 * P], BF16)
            self.before = keep("before", [P, P], BF16)
            self.onesb = keep("onesb", [P, P], BF16)
            self.expert_w = keep("expert_w", [P, 2, DK * 2 * FF + 2 * D])
            self.who = keep("who", [P, NBMAX], I32)
            self.where = keep("where", [P, NBMAX], I32)
            self.gates = keep("gates", [P, NBMAX])
            self.ends_i = keep("ends_i", [1, NE + 1], I32)
            self.ps = self.ctx.enter_context(nc.psum_tensor("ps", [P, 4096], F32))
            self.tick = self.ctx.enter_context(nc.semaphore("tick_pool"))
            self.tick_pe = self.ctx.enter_context(nc.semaphore("tick_pe"))
            self.tick_sp = self.ctx.enter_context(nc.semaphore("tick_sp"))
            self.weights_in = [self.ctx.enter_context(nc.semaphore(f"weights_in{i}")) for i in range(8)]
            self.expert_in = [[self.ctx.enter_context(nc.semaphore(f"expert_in{l}{i}")) for i in range(2)]
                              for l in range(2)]
            self.rope_d = self.dram("rope_d", [T, ROT])
            self.q_d = self.dram("q_d", [T, D])
            self.k_d = self.dram("k_d", [T, DW])
            self.v_d = self.dram("v_d", [T, DW])
            self.a_d = self.dram("a_d", [T, SGU])
            self.o_d = self.dram("o_d", [T, 3 * (QUAD + 8)])
            self.k1_d = self.dram("k1_d", [T, 4 * HD])
            self.v1_d = self.dram("v1_d", [T, 2 * HD])
            self.o1_d = self.dram("o1_d", [T, D])
            self.h_d = [self.dram("h_d", [T + P, D]), self.out]
            self.hn_d = [self.dram(f"hn{i}_d", [T, D]) for i in range(2)]
            self.lg_d = [self.dram(f"lg{i}_d", [T, NL]) for i in range(2)]
            flat = self.expert_w[:, :, :].rearrange("p s c -> p (s c)")
            slots = flat.rearrange("p (s k n) -> p s k n", s=3, k=DK)
            even = self.x["w_in_even"].rearrange("a (p k) n -> p (a k) n", k=DK)
            self.w_in_qk = flat.rearrange("p (k n) -> p k n", k=DK)
            self.w_in_odd = flat[:, 0:DK * 1280].rearrange("p (k n) -> p k n", k=DK)
            self.pieces = {
                "gate": [(even[:, :, c:c + n], slots[:, i % 3, :, 0:n], at, n, self.weights_in[i])
                         for i, (c, at, n) in enumerate(((0, 0, 512), (512, 512, 512), (2560, 1024, 384), (2944, 1408, 384)))],
                "qk": [(None, self.w_in_qk[:, :, c:c + 512], c, 512, self.weights_in[4]) for c in (0, 512, 1024)],
                "all": [(None, self.w_in_odd[:, :, c:c + n], c, n, self.weights_in[5]) for c, n in ((0, 512), (512, 512), (1024, 256))],
            }
            setup(self)
            project_in(self, "gate")
            project_in(self, "qk")
            for layer in range(2):
                with nc.sbuf_tensor(f"out_w{layer}", [P, 8 * D], F32) as self.out_w:
                    NK = (6, DK)[layer]
                    self.w_out = self.out_w[:, 0:NK * D].rearrange("p (k n) -> p k n", k=NK)
                    if layer == 1:
                        project_in(self, "all")
                    attend(self, layer)
                    project_out(self, layer)
                    route(self, layer)
                experts(self, layer)


def setup(K):
    nc, ps = K.nc, K.ps
    with K.phase("s") as (sb, sem, block):
        pos_i = sb("pos_i", [P, NT], I32)
        pos = sb("pos", [P, NT])
        inv = sb("inv", [P, HALF])
        ang = sb("ang", [P, NT, HALF])
        turns = sb("turns", [P, NT, HALF])
        rest = sb("rest", [P, NT, HALF])
        table = sb("table", [P, NT, ROT])
        quarter = sb("quarter", [P, 1])
        zeros = sb("zeros", [P, D])
        pos_in, own, tab, sin_done, stored, made = (sem(n) for n in
            ("pos_in", "own", "tab", "sin_done", "stored", "made"))
        pool_own = sem("pool_own")

        @block.sync
        def _(sp):
            with nc.allow_non_contiguous_dma("2048 positions, once"):
                sp.dma_start(pos_i[:, :], K.x["positions"].rearrange("a (n p) -> p (a n)", p=P)).then_inc(pos_in, 16)
            src, place, _, _, there = K.pieces["gate"][0]
            sp.dma_start(place, src).then_inc(there, 16)
            sp.wait_ge(made, 1)
            for h in K.h_d:
                sp.dma_start(h[T:T + P, :], zeros[:, :]).then_inc(stored, 16)
            sp.wait_ge(sin_done, 2)
            sp.dma_start(K.rope_d.rearrange("(n p) c -> p n c", p=P), table[:, :, :]).then_inc(stored, 16)
            sp.wait_ge(stored, 48)

        @block.gpsimd
        def _(g):
            own_ = Chain(g, pool_own)
            for t in (K.ident, K.identb):
                own_.link(g.memset(t[:, :], 0.0))
                own_.link(g.affine_select(out=t[:, :], in_=t[:, :], compare_op=ALU.not_equal, fill=1.0,
                                          base=0, pattern=[[-1, P]], channel_multiplier=1))
            own_.link(g.memset(K.masks[:, :, :], 0.0))
            for m, (base, mult) in enumerate(((0, -1), (-1, -1), (-P, 0))):
                for b, c, s in ((base, mult, 1), (P, 1, -1)):
                    own_.link(g.affine_select(out=K.masks[:, m, :], in_=K.masks[:, m, :], compare_op=ALU.is_ge,
                                              fill=NEG, base=b, pattern=[[s, 2 * P]], channel_multiplier=c))
            own_.link(g.memset(K.onesb[:, :], 1.0))
            own_.link(g.affine_select(out=K.before[:, :], in_=K.onesb[:, :], compare_op=ALU.is_ge, fill=0.0,
                                      base=-1, pattern=[[1, P]], channel_multiplier=-1))
            own_.link(g.memset(zeros[:, :], 0.0))
            g.sem_inc(made, 1)

        @block.vector
        def _(v):
            own_ = Chain(v, own)
            v.wait_ge(pos_in, 16)
            own_.link(nc.vector.tensor_copy(pos[:, :], pos_i[:, :]))
            own_.link(nc.vector.memset(quarter[:, :], np.pi / 2))
            for c in range(HALF):
                own_.link(nc.vector.memset(inv[:, c:c + 1], float(np.float32(THETA) ** np.float32(-2.0 * c / ROT))))
            shape = [P, NT, HALF]
            own_.link(nc.vector.tensor_tensor(ang[:, :, :], pos[:, :].unsqueeze(2).broadcast_to(shape),
                                              inv[:, :].unsqueeze(1).broadcast_to(shape), ALU.mult))
            magic = 1.5 * 2.0 ** 23
            own_.link(nc.vector.tensor_scalar(turns[:, :, :], ang[:, :, :], float(1 / (2 * np.pi)), magic, ALU.mult, ALU.add))
            own_.link(nc.vector.tensor_scalar(turns[:, :, :], turns[:, :, :], magic, None, ALU.subtract))
            own_.link(nc.vector.tensor_copy(rest[:, :, :], ang[:, :, :]))
            left = 2 * np.pi
            for bits in (7, 16, 25, 60):
                part = np.floor(left * 2.0 ** bits) / 2.0 ** bits if bits < 60 else left
                left -= part
                own_.link(nc.vector.scalar_tensor_tensor(rest[:, :, :], turns[:, :, :], -float(part), rest[:, :, :],
                                                         ALU.mult, ALU.add))
            own_.link(nc.vector.tensor_scalar(rest[:, :, :], rest[:, :, :], 3.1415925, -3.1415925, ALU.min, ALU.max))
            nc.vector.scalar_tensor_tensor(ang[:, :, :], rest[:, :, :], -1.0, rest[:, :, :], ALU.mult, ALU.max).then_inc(tab, 1)

        @block.scalar
        def _(a):
            a.wait_ge(tab, 1)
            nc.scalar.activation(table[:, :, 0:HALF], ang[:, :, :], ACT.Sin, scale=-1.0, bias=quarter[:, 0:1]).then_inc(sin_done, 1)
            nc.scalar.activation(table[:, :, HALF:ROT], rest[:, :, :], ACT.Sin).then_inc(sin_done, 1)


def project_in(K, part):
    nc, ps = K.nc, K.ps
    even, gating, qk_too, val_too = part != "all", part == "gate", part != "gate", part != "qk"
    layer = 0 if even else 1
    pieces = K.pieces[part]
    groups = [(c0, wd) for _, _, c0, wd, _ in pieces]
    G = len(groups)
    NQK = 2 * NDH if even else 18
    NQ = NDH if even else 16
    QKW = NQK * HD
    VW = DW if even else 2 * HD
    nb = 1 if gating else 2
    stores = 4 if part == "all" else 2

    with K.phase(f"in_{part}") as (sb, sem, block):
        w = sb("w", [P, 2, DK, sum(wd for _, wd in groups)], F32R)
        xt = sb("xt", [P, 2, D])
        hnT = sb("hnT", [P, 2, 2, DK, P], F32R)
        gain = sb("gain", [P, D])
        ssx, rx = sb("ssx", [P, 2, 2]), sb("rx", [P, 2])
        power = sb("power", [P, 1])
        if qk_too:
            cs = sb("cs", [P, 2, ROT])
            qk_gain = sb("qk_gain", [P, 2, HD])
            qk_ = sb("qk", [P, nb, QKW])
            sq = sb("sq", [P, QKW])
            ssq, rq = sb("ssq", [P, NQK]), sb("rq", [P, NQK])
            rot = sq[:, 0:4 * NQK * HALF].rearrange("p (r h c) -> p r h c", r=4, h=NQK)
        if gating:
            u, v = sb("u", [P, SGU]), sb("v", [P, SGU])
            av = sb("av", [P, SGU])
            v_gain = sb("v_gain", [P, SGU])
            ssv, rv = sb("ssv", [P, 1]), sb("rv", [P, 1])
            ws = sb("ws", [P, SG, P])
            bs, bsT = sb("bs", [SG, P]), sb("bsT", [P, SG])
        val_ = sb("val", [P, nb, VW]) if val_too else None
        x_in, cs_in = [sem("x_in0"), sem("x_in1")], [sem("cs_in0"), sem("cs_in1")]
        par_in, st, own, pool_own = sem("par_in"), sem("st"), sem("own"), sem("pool_own")
        w_high, w_low = sem("w_high"), sem("w_low")
        xn_done, roped = Count(sem("xn_done"), 2), Count(sem("roped"))
        sum_x, rms_x = Count(sem("sum_x"), 1), Count(sem("rms_x"), 2)
        sum_q, rms_q = Count(sem("sum_q")), Count(sem("rms_q"))
        sum_v, rms_v = Count(sem("sum_v")), Count(sem("rms_v"))
        turned, x_high, x_low = Count(sem("turned"), 2), Count(sem("x_high")), Count(sem("x_low"), 1)
        grp, act_out = Count(sem("grp")), Count(sem("act_out"), G)
        stored = Count(sem("stored"), nb)
        vn_done, mixed, gated = Count(sem("vn_done")), Count(sem("mixed")), Count(sem("gated"), 1)
        ready, power_set = sem("ready"), sem("power_set")
        ws_turned, ws_out = sem("ws_turned"), sem("ws_out")
        params = 1 + 2 * qk_too + 3 * gating
        tp = ps[:, 0:D]
        junk = ps[:, 3584:4096]
        mix = ps[:, 3072:3072 + SGU]

        def bank(gi):
            return ps[:, 1024 + 512 * gi:1024 + 512 * gi + groups[gi][1]]

        @block.sync
        def _(sp):
            def load(s):
                j, n = s.slot(2), s.n
                alone(sp, turned, n - 1, K.tick_sp)
                src = K.x["x"].rearrange("a t c -> (a t) c") if even else K.h_d[0][0:T]
                sp.dma_start(xt[:, j, :], rows(src, n)).then_inc(x_in[j], 16)

            def load_cs(s):
                sp.dma_start(cs[:, s.slot(2), :], rows(K.rope_d, s.n)).then_inc(cs_in[s.slot(2)], 16)

            def store(s):
                issue(s)
                sp.wait_ge(st, s.n * (16 * stores) + 16 * stores)
                sp.sem_inc(stored.sem, 1)

            def issue(s):
                b, n = s.slot(nb), s.n
                if gating:
                    alone(sp, act_out, n * G + G, K.tick_sp)
                    sp.dma_start(rows(K.v_d, n), val_[:, b, :]).then_inc(st, 16)
                    alone(sp, gated, n + 1, K.tick_sp)
                    sp.dma_start(rows(K.a_d, n), av[:, :]).then_inc(st, 16)
                    return
                alone(sp, roped, n + 1, K.tick_sp)
                sp.dma_start(rows(K.q_d[:, 0:NQ * HD], n), qk_[:, b, 0:NQ * HD]).then_inc(st, 16)
                if even:
                    sp.dma_start(rows(K.k_d, n), qk_[:, b, DW:2 * DW]).then_inc(st, 16)
                    return
                for dup in range(2):
                    sp.dma_start(rows(K.k1_d, n).rearrange("p (h d c) -> p h d c", h=2, d=2)[:, :, dup, :],
                                 qk_[:, b, D:D + 2 * HD].rearrange("p (h c) -> p h c", h=2)).then_inc(st, 16)
                sp.dma_start(rows(K.v1_d, n), val_[:, b, :]).then_inc(st, 16)

            def step(s):
                if s.plus(2).within(NT):
                    load(s.plus(2))
                if gating:
                    store(s)
                elif not isinstance(s.n, int) or s.n >= 1:
                    store(s.plus(-1))
                    if s.plus(1).within(NT):
                        load_cs(s.plus(1))
            sp.sem_inc(stored.sem, stored.credit)
            sp.wait_ge(ready, 1)
            s0, s1 = Step(0, 0, 2), Step(0, 1, 2)
            load(s0)
            sp.dma_start(gain[:, :], K.x["norm_mix"][layer:layer + 1].broadcast_to([P, D])).then_inc(par_in, 16)
            if qk_too:
                for i, name in enumerate(("qn_dil", "kn_dil") if even else ("qn_swa", "kn_swa")):
                    sp.dma_start(qk_gain[:, i, :], K.x[name].broadcast_to([P, HD])).then_inc(par_in, 16)
                load_cs(s0)
                load_cs(s1)
            if gating:
                sp.dma_start(v_gain[:, :], K.x["sgu_norm"].broadcast_to([P, SGU])).then_inc(par_in, 16)
                sp.dma_start(ws[:, :, :], K.x["sgu_w"].rearrange("a g t c -> t (a g) c")).then_inc(par_in, 16)
                sp.dma_start(bs[:, :], K.x["sgu_b"].rearrange("a g t -> (a g) t")).then_inc(par_in, 16)
            load(s1)
            if gating:
                for n, (src, place, _, _, there) in enumerate(pieces[1:]):
                    if n == 2:
                        sp.wait_ge(w_low, 1)
                    sp.dma_start(place, src).then_inc(there, 16)
                sp.wait_ge(w_low, G)
                sp.dma_start(K.w_in_qk, K.x["w_in_even"].rearrange("a (p k) n -> p (a k) n", k=DK)[:, :, 2 * SGU:2 * SGU + 2 * DW]
                             ).then_inc(K.weights_in[4], 16)
            if not even:
                sp.dma_start(K.w_out, K.x["w_out_odd"].rearrange("a (p k) n -> p (a k) n", k=DK)).then_inc(K.weights_in[7], 16)
            looped(sp, NT, 2, 2, step, head=1)
            if qk_too:
                store(Step(NT // 2 - 1, 1, 2))

        @block.scalar
        def _(a):
            def square(s):
                j = s.slot(2)
                a.wait_ge(x_in[j], s.turn(2) * 16 + 16)
                until(a, rms_x, s.n - 1)
                for half in range(2):
                    until(a, sum_x, s.n * 2 + half)
                    nc.scalar.activation(junk, xt[:, j, 512 * half:512 * (half + 1)], ACT.Square,
                                         accum_out=ssx[:, j, half:half + 1]).then_inc(sum_x.sem, 1)

            def turn_out(s):
                until(a, turned, s.n + 1)
                nc.scalar.activation(hnT[:, s.slot(2), 0, :, :], tp.rearrange("p (k c) -> p k c", k=DK), ACT.Copy).then_inc(x_high.sem, 1)

            def group_out(s, gi):
                c0, wd = groups[gi]
                b = s.slot(nb)
                until(a, grp, s.n * G + gi + 1)
                if gating and gi < 2:
                    if gi == 0:
                        until(a, gated, s.n)
                    nc.scalar.activation((u, v)[gi][:, :], bank(gi), ACT.Gelu_apprx_tanh).then_inc(act_out.sem, 1)
                    return
                if gi == (2 if gating else 0):
                    until(a, stored, s.n - nb + 1)
                if gating:
                    nc.scalar.activation(val_[:, b, c0 - 2 * SGU:c0 - 2 * SGU + wd], bank(gi), ACT.Copy).then_inc(act_out.sem, 1)
                elif not even and gi == 2:
                    nc.scalar.activation(qk_[:, b, D:D + 2 * HD], bank(gi)[:, 0:2 * HD], ACT.Copy)
                    nc.scalar.activation(val_[:, b, :], bank(gi)[:, 2 * HD:4 * HD], ACT.Copy).then_inc(act_out.sem, 1)
                else:
                    nc.scalar.activation(qk_[:, b, c0:c0 + wd], bank(gi), ACT.Copy).then_inc(act_out.sem, 1)

            def step(s):
                if s.plus(1).within(NT):
                    square(s.plus(1))
                group_out(s, 0)
                group_out(s, 1)
                if s.plus(1).within(NT):
                    turn_out(s.plus(1))
                for gi in range(2, G):
                    group_out(s, gi)
            a.sem_inc(act_out.sem, act_out.credit)
            a.sem_inc(sum_x.sem, sum_x.credit)
            square(Step(0, 0, 2))
            turn_out(Step(0, 0, 2))
            for _, place, c0, wd, there in pieces:
                a.wait_ge(there, 16)
                nc.scalar.activation(w[:, 0, :, c0:c0 + wd], place, ACT.Copy).then_inc(w_high, 1)
            looped(a, NT, 2, 2, step)

        @block.gpsimd
        def _(g):
            own_ = Chain(g, pool_own, K.tick)
            own_.link(g.memset(power[:, :], -0.5))
            g.sem_inc(rms_x.sem, rms_x.credit)

            def rms(own_, out, total, width, done):
                own_.link(g.tensor_scalar(out, total, 1.0 / width, EPS, ALU.mult, ALU.add))
                g.tensor_tensor(out, out, power[:, 0:1].broadcast_to([P, out.shape[1]]), ALU.pow).then_inc(done.sem, 1)

            def rms_tile(s):
                j = s.slot(2)
                alone(g, sum_x, s.n * 2 + 2, K.tick)
                alone(g, xn_done, s.n - 1, K.tick)
                own_.link(g.tensor_tensor(rx[:, j:j + 1], ssx[:, j, 0:1], ssx[:, j, 1:2], ALU.add))
                rms(own_, rx[:, j:j + 1], rx[:, j:j + 1], D, rms_x)

            def rms_heads(s):
                alone(g, sum_q, s.n + 1, K.tick)
                rms(own_, rq[:, :], ssq[:, :], HD, rms_q)

            def step(s):
                if s.plus(1).within(NT):
                    rms_tile(s.plus(1))
                if gating:
                    alone(g, sum_v, s.n + 1, K.tick)
                    rms(own_, rv[:, :], ssv[:, :], SGU, rms_v)
                elif not isinstance(s.n, int) or s.n >= 1:
                    rms_heads(s.plus(-1))
            rms_tile(Step(0, 0, 2))
            if gating:
                g.wait_ge(ws_out, SG)
                own_.link(g.affine_select(out=ws[:, :, :], in_=ws[:, :, :], compare_op=ALU.is_ge, fill=0.0,
                                          base=0, pattern=[[0, SG], [1, P]], channel_multiplier=-1))
                g.sem_inc(power_set, 1)
            looped(g, NT, 2, 2, step, own_, 3, head=1)
            if qk_too:
                rms_heads(Step(NT // 2 - 1, 1, 2))

        @block.tensor
        def _(pe):
            def turn(s):
                until(pe, xn_done, s.n + 1)
                until(pe, x_low, s.n)
                src = xt[:, s.slot(2), :].rearrange("p (c k) -> p k c", k=DK)
                for k in range(DK):
                    last = nc.tensor.transpose(tp[:, k * P:(k + 1) * P], src[:, k, :], K.ident[:, :])
                last.then_inc(turned.sem, 1)

            def group(s, gi):
                c0, wd = groups[gi]
                until(pe, act_out, (s.n - 1) * G + gi + 1)
                pe.wait_ge(w_low, gi + 1)
                for a, b in ((0, 0), (0, 1), (1, 0)):
                    if a == 1 and gi == 0:
                        until(pe, x_low, s.n + 1)
                    for k in range(DK):
                        last = nc.tensor.matmul(bank(gi), hnT[:, s.slot(2), a, k, :], w[:, b, k, c0:c0 + wd],
                                                start=(a + b + k == 0), stop=(a == 1 and k == DK - 1))
                last.then_inc(grp.sem, 1)

            def step(s):
                until(pe, x_high, s.n + 1)
                group(s, 0)
                group(s, 1)
                if s.plus(1).within(NT):
                    turn(s.plus(1))
                for gi in range(2, G):
                    group(s, gi)
                if gating:
                    until(pe, vn_done, s.n + 1)
                    until(pe, gated, s.n)
                    for c in range(SG):
                        mm = nc.tensor.matmul(mix[:, c * HD:(c + 1) * HD], ws[:, c, :], v[:, c * HD:(c + 1) * HD],
                                              start=True, stop=True)
                    mm.then_inc(mixed.sem, 1)
            pe.sem_inc(turned.sem, turned.credit)
            turn(Step(0, 0, 2))
            if gating:
                pe.wait_ge(par_in, 16 * params)
                for c in range(SG):
                    nc.tensor.transpose(ps[:, 1024 + c * P:1024 + (c + 1) * P], ws[:, c, :], K.ident[:, :]).then_inc(ws_turned, 1)
                nc.tensor.transpose(ps[:, 3072:3072 + SG], bs[:, :], K.ident[0:SG, 0:SG]).then_inc(ws_turned, 1)
                pe.wait_ge(ws_out, SG + 1)
                pe.wait_ge(power_set, 1)
            looped(pe, NT, 2, 2, step)

        @block.vector
        def _(v_):
            own_ = Chain(v_, own)
            for c in (xn_done, gated, x_low):
                v_.sem_inc(c.sem, c.credit)
            v_.sem_inc(ready, 1)

            def norm(s):
                j = s.slot(2)
                until(v_, rms_x, s.n + 1)
                nc.vector.scalar_tensor_tensor(xt[:, j, :], xt[:, j, :], rx[:, j:j + 1], gain[:, :], ALU.mult, ALU.mult).then_inc(xn_done.sem, 1)

            def turn_out(s):
                j = s.slot(2)
                until(v_, x_high, s.n + 1)
                nc.vector.tensor_tensor(hnT[:, j, 1, :, :], tp.rearrange("p (k c) -> p k c", k=DK),
                                        hnT[:, j, 0, :, :].bitcast(F32), ALU.subtract).then_inc(x_low.sem, 1)

            def square_heads(s):
                until(v_, act_out, s.n * G + G)
                qk = qk_[:, s.slot(nb), :]
                own_.link(nc.vector.tensor_tensor(sq[:, :], qk, qk, ALU.mult))
                nc.vector.tensor_reduce(ssq[:, :], sq[:, :].rearrange("p (h c) -> p h c", c=HD), AX, ALU.add).then_inc(sum_q.sem, 1)

            def norm_rotate(s):
                heads = qk_[:, s.slot(nb), :].rearrange("p (h c) -> p h c", c=HD)
                until(v_, rms_q, s.n + 1)
                own_.link(nc.vector.tensor_tensor(heads, heads, rq[:, :].unsqueeze(2).broadcast_to([P, NQK, HD]), ALU.mult))
                own_.mark(nc.vector.tensor_tensor(heads[:, 0:NQ, :], heads[:, 0:NQ, :],
                                                  qk_gain[:, 0, :].unsqueeze(1).broadcast_to([P, NQ, HD]), ALU.mult))
                own_.link(nc.vector.tensor_tensor(heads[:, NQ:NQK, :], heads[:, NQ:NQK, :],
                                                  qk_gain[:, 1, :].unsqueeze(1).broadcast_to([P, NQK - NQ, HD]), ALU.mult))
                j = s.slot(2)
                v_.wait_ge(cs_in[j], s.turn(2) * 16 + 16)
                wide = [P, NQK, HALF]
                cos = cs[:, j, 0:HALF].unsqueeze(1).broadcast_to(wide)
                sin = cs[:, j, HALF:ROT].unsqueeze(1).broadcast_to(wide)
                x1, x2 = heads[:, :, 0:HALF], heads[:, :, HALF:ROT]
                own_.mark(nc.vector.tensor_tensor(rot[:, 0, :, :], x1, cos, ALU.mult))
                own_.mark(nc.vector.tensor_tensor(rot[:, 1, :, :], x2, sin, ALU.mult))
                own_.mark(nc.vector.tensor_tensor(rot[:, 2, :, :], x2, cos, ALU.mult))
                own_.link(nc.vector.tensor_tensor(rot[:, 3, :, :], x1, sin, ALU.mult))
                own_.mark(nc.vector.tensor_tensor(x1, rot[:, 0, :, :], rot[:, 1, :, :], ALU.subtract))
                own_.link(nc.vector.tensor_tensor(x2, rot[:, 2, :, :], rot[:, 3, :, :], ALU.add))
                v_.sem_inc(roped.sem, 1)

            def v_norm(s):
                until(v_, act_out, s.n * G + 2)
                until(v_, stored, s.n)
                own_.link(nc.vector.tensor_tensor(av[:, :], v[:, :], v[:, :], ALU.mult))
                nc.vector.tensor_reduce(ssv[:, :], av[:, :], AX, ALU.add).then_inc(sum_v.sem, 1)
                until(v_, rms_v, s.n + 1)
                nc.vector.scalar_tensor_tensor(v[:, :], v[:, :], rv[:, 0:1], v_gain[:, :], ALU.mult, ALU.mult).then_inc(vn_done.sem, 1)

            def gate(s):
                until(v_, mixed, s.n + 1)
                own_.link(nc.vector.tensor_tensor(av[:, :].rearrange("p (c d) -> p c d", c=SG),
                                                  mix.rearrange("p (c d) -> p c d", c=SG),
                                                  bsT[:, :].unsqueeze(2).broadcast_to([P, SG, HD]), ALU.add))
                nc.vector.tensor_tensor(av[:, :], av[:, :], u[:, :], ALU.mult).then_inc(gated.sem, 1)

            def step(s):
                heads_too = qk_too and (not isinstance(s.n, int) or s.n >= 1)
                if heads_too:
                    square_heads(s.plus(-1))
                if s.plus(1).within(NT):
                    norm(s.plus(1))
                if gating:
                    v_norm(s)
                if heads_too:
                    norm_rotate(s.plus(-1))
                if s.plus(1).within(NT):
                    turn_out(s.plus(1))
                if gating:
                    gate(s)
            v_.wait_ge(par_in, 16 * params)
            norm(Step(0, 0, 2))
            if gating:
                v_.wait_ge(ws_turned, SG + 1)
                for c in range(SG):
                    nc.vector.tensor_copy(ws[:, c, :], ps[:, 1024 + c * P:1024 + (c + 1) * P]).then_inc(ws_out, 1)
                nc.vector.tensor_copy(bsT[:, :], ps[:, 3072:3072 + SG]).then_inc(ws_out, 1)
            turn_out(Step(0, 0, 2))
            for n, (_, place, c0, wd, _) in enumerate(pieces):
                v_.wait_ge(w_high, n + 1)
                nc.vector.tensor_tensor(w[:, 1, :, c0:c0 + wd], place, w[:, 0, :, c0:c0 + wd].bitcast(F32),
                                        ALU.subtract).then_inc(w_low, 1)
            looped(v_, NT, 2, 2, step, own_, 2 if gating else 10, head=1)
            if qk_too:
                square_heads(Step(NT // 2 - 1, 1, 2))
                norm_rotate(Step(NT // 2 - 1, 1, 2))


def attend(K, layer):
    nc, ps = K.nc, K.ps
    even = layer == 0
    U = 4
    N = 3 * NT if even else 4 * NT
    OW = QUAD + 8 if even else QUAD
    KH = 4 if even else 2
    VH = 4 if even else 1
    NTP = 2 + KH
    with K.phase(f"att{layer}") as (sb, sem, block):
        q = sb("q", [P, U, QUAD])
        k = sb("k", [P, U, 2, KH * HD])
        v = sb("v", [P, U, 2, VH * HD])
        mask = sb("mask", [P, U, 2 * P], BF16)
        turned_sb = sb("turned_sb", [P, 2, NTP * P])
        probs = sb("probs", [P, 2, 4, 2 * P])
        probsT = sb("probsT", [P, 2, 8, P])
        outs = sb("outs", [P, U, OW])
        mx, negm = sb("mx", [P, 2, 4]), sb("negm", [P, 2, 4])
        den, rden, sink_e = sb("den", [P, U, 4]), sb("rden", [P, U, 4]), sb("sink_e", [P, U, 4])
        sinks = sb("sinks", [P, 16])
        qk_in, v_in = [sem(f"qk_in{i}") for i in range(U)], [sem(f"v_in{i}") for i in range(U)]
        turned, turned_out = Count(sem("turned"), U), Count(sem("turned_out"), 1)
        scored, lowered = Count(sem("scored"), U), Count(sem("lowered"))
        exped, p_turned, p_out = Count(sem("exped"), 2), Count(sem("p_turned"), 2), [Count(sem("p_out0"), 1), Count(sem("p_out1"), 1)]
        summed, o_out, stored = Count(sem("summed"), U), Count(sem("o_out"), 2), Count(sem("stored"), U)
        st, own, sinks_in, sunk = sem("st"), sem("own"), sem("sinks_in"), Count(sem("sunk"))
        tp = ps[:, 0:NTP * P]
        op = ps[:, D - QUAD:D]
        sc = ps[:, 1024:3072].rearrange("p (b x y c) -> p b x y c", b=2, x=2, y=2)
        pp = ps[:, 3072:4096].rearrange("p (t c) -> p t c", c=P)

        def span(ap, dil, r, l0, c0, width):
            v_ = ap.rearrange("(l d) c -> d l c", d=dil)
            if not isinstance(r, int):
                return v_[bass.ds(r, 1), l0:l0 + P, c0:c0 + width].rearrange("d l c -> (d l) c")
            v_ = v_[r]
            return (v_[l0:l0 + P] if isinstance(l0, int) else v_[bass.ds(l0, P)])[:, c0:c0 + width]

        def walk(eng, visit):
            if even:
                visit(0, 0, 1, 0, 0, 0, True)
                for j in (1, 2, 3):
                    visit(j, j, 1, 0, j, 0, False)
                with eng.Fori(1, 4) as i:
                    for j in range(4):
                        visit(j, i * 4 + j, 1, 0, i * 4 + j, 0, False)
                for r in range(4):
                    visit(r, 16 + r, 4, r, 0, 1, True)
                with eng.Fori(1, 4) as b:
                    for r in range(4):
                        visit(r, b * 4 + (16 + r), 4, r, b, 1, False)
                with eng.Fori(0, 4) as i:
                    for j in range(4):
                        visit(j, i * 4 + (32 + j), 16, i * 4 + j, 0, 2, True)
            else:
                for j in range(4):
                    visit(j, j, 1, 0, 0, j, True)
                with eng.Fori(1, NT) as b:
                    for j in range(4):
                        visit(j, b * 4 + j, 1, 0, b, j, False)

        @block.sync
        def _(sp):
            if not even:
                sp.dma_start(sinks[:, :], K.x["sinks"].broadcast_to([P, 16])).then_inc(sinks_in, 16)
            if even:
                sp.dma_start(K.w_out, K.x["w_out_even"].rearrange("a (p k) n -> p (a k) n", k=6)).then_inc(K.weights_in[6], 16)

            def load(j, n, dil, r, b, g, first):
                alone(sp, turned, n - 3, K.tick_sp)
                alone(sp, scored, n - 3, K.tick_sp)
                kc, vc = (g * QUAD, g * QUAD) if even else ((g // 2) * 2 * HD, (g // 2) * HD)
                kd, vd = (K.k_d, K.v_d) if even else (K.k1_d, K.v1_d)
                l0 = b * P
                before = l0 if first else l0 - P
                sp.dma_start(q[:, j, :], span(K.q_d, dil, r, l0, g * QUAD, QUAD)).then_inc(qk_in[j], 16)
                for half, at in enumerate((before, l0)):
                    sp.dma_start(k[:, j, half, :], span(kd, dil, r, at, kc, KH * HD)).then_inc(qk_in[j], 16)
                m = 2 if first else (0 if even else 1)
                sp.dma_start(mask[:, j, :], K.masks[:, m, :]).then_inc(qk_in[j], 16)
                alone(sp, summed, n - 3, K.tick_sp)
                for half, at in enumerate((before, l0)):
                    sp.dma_start(v[:, j, half, :], span(vd, dil, r, at, vc, VH * HD)).then_inc(v_in[j], 16)
            walk(sp, load)

        @block.gpsimd
        def _(g_):
            g_.sem_inc(stored.sem, stored.credit)

            def store(j, n, dil, r, b, g, first):
                alone(g_, o_out, n + 1, K.tick)
                if even:
                    dst = span(K.o_d, dil, r, b * P, g * OW, OW)
                else:
                    dst = span(K.o1_d, dil, r, b * P, g * QUAD, QUAD)
                g_.dma_start(dst, outs[:, j, :]).then_inc(st, 16)
                g_.wait_ge(st, n * 16 + 16)
                g_.sem_inc(stored.sem, 1)
            walk(g_, store)

        @block.tensor
        def _(pe):
            for c in (turned, scored, p_turned, summed):
                pe.sem_inc(c.sem, c.credit)

            def turn(s):
                j = s.slot(U)
                pe.wait_ge(qk_in[j], s.turn(U) * 64 + 64)
                until(pe, turned_out, s.n)
                if even and (not isinstance(s.n, int) or s.n >= 4):
                    until(pe, o_out, s.n - 3)
                for t in range(2):
                    nc.tensor.transpose(tp[:, t * P:(t + 1) * P], q[:, j, t * P:(t + 1) * P], K.ident[:, :])
                for pair in range(KH // 2):
                    for half in range(2):
                        at = (2 + 2 * pair + half) * P
                        last = nc.tensor.transpose(tp[:, at:at + P], k[:, j, half, pair * P:(pair + 1) * P], K.ident[:, :])
                last.then_inc(turned.sem, 1)

            def score(s):
                b = s.slot(2)
                until(pe, turned_out, s.n + 1)
                until(pe, exped, s.n - 1)
                qkT = turned_sb[:, b, :]
                for x in range(2):
                    nc.tensor.matmul(sc[:, b, x, :, :], K.identb[:, :],
                                     mask[:, s.slot(U), :].unsqueeze(1).broadcast_to([P, 2, 2 * P]), start=True, stop=False)
                for h in range(4):
                    lo = HD * (h % 2)
                    kp = h // 2 if even else 0
                    last = nc.tensor.matmul(sc[:, b, h % 2, h // 2, :], qkT[lo:lo + HD, (h // 2) * P:(h // 2 + 1) * P],
                                            qkT[lo:lo + HD, (2 + 2 * kp) * P:(4 + 2 * kp) * P], start=False, stop=(h >= 2))
                last.then_inc(scored.sem, 1)

            def turn_probs(s):
                until(pe, exped, s.n + 1)
                until(pe, p_out[0], s.n)
                until(pe, p_out[1], s.n)
                for h in range(4):
                    for half in range(2):
                        last = nc.tensor.transpose(pp[:, 2 * h + half, :], probs[:, s.slot(2), h, half * P:(half + 1) * P],
                                                   K.ident[:, :])
                last.then_inc(p_turned.sem, 1)

            def weigh(s):
                pe.wait_ge(v_in[s.slot(U)], s.turn(U) * 32 + 32)
                until(pe, o_out, s.n)
                if even and s.plus(3).within(N):
                    until(pe, turned_out, s.n + 4)
                for h in range(4):
                    if h % 2 == 0:
                        until(pe, p_out[h // 2], s.n + 1)
                    vh = h if even else 0
                    for half in range(2):
                        last = nc.tensor.matmul(op[:, h * HD:(h + 1) * HD], probsT[:, s.slot(2), 2 * h + half, :],
                                                v[:, s.slot(U), half, vh * HD:(vh + 1) * HD],
                                                start=(half == 0), stop=(half == 1))
                last.then_inc(summed.sem, 1)

            def step(s):
                if s.plus(1).within(N):
                    score(s.plus(1))
                if s.plus(2).within(N):
                    turn(s.plus(2))
                turn_probs(s)
                if not isinstance(s.n, int) or s.n >= 1:
                    weigh(s.plus(-1))
            s0 = Step(0, 0, U)
            turn(s0)
            score(s0)
            turn(s0.plus(1))
            looped(pe, N, U, U, step, head=1)
            weigh(Step(N // U - 1, U - 1, U))

        @block.scalar
        def _(a):
            for c in (exped, turned_out, p_out[1]):
                a.sem_inc(c.sem, c.credit)

            def exps(s):
                b = s.slot(2)
                until(a, lowered, s.n + 1)
                until(a, p_turned, s.n - 1)
                if not even:
                    nc.scalar.activation(sink_e[:, s.slot(U), :], sink_e[:, s.slot(U), :], ACT.Exp).then_inc(sunk.sem, 1)
                for h in range(4):
                    total = outs[:, s.slot(U), QUAD + 4 + h:QUAD + 5 + h] if even else den[:, s.slot(U), h:h + 1]
                    last = nc.scalar.activation(probs[:, b, h, :], sc[:, b, h % 2, h // 2, :], ACT.Exp, bias=negm[:, b, h:h + 1],
                                                scale=SCALE, accum_out=total)
                last.then_inc(exped.sem, 1)

            def turn_out(s):
                until(a, turned, s.n + 1)
                until(a, scored, s.n - 1)
                nc.scalar.activation(turned_sb[:, s.slot(2), :], tp, ACT.Copy).then_inc(turned_out.sem, 1)

            def step(s):
                if s.plus(2).within(N):
                    turn_out(s.plus(2))
                until(a, p_turned, s.n + 1)
                until(a, summed, s.n - 1)
                nc.scalar.activation(probsT[:, s.slot(2), 4:8, :], pp[:, 4:8, :], ACT.Copy).then_inc(p_out[1].sem, 1)
                if s.plus(1).within(N):
                    exps(s.plus(1))
            s0 = Step(0, 0, U)
            turn_out(s0)
            turn_out(s0.plus(1))
            exps(s0)
            looped(a, N, U, U, step)

        @block.vector
        def _(v_):
            own_ = Chain(v_, own)
            for c in (o_out, p_out[0]):
                v_.sem_inc(c.sem, c.credit)
            if not even:
                v_.wait_ge(sinks_in, 16)

            def probs_out(s):
                until(v_, p_turned, s.n + 1)
                until(v_, summed, s.n - 1)
                nc.vector.tensor_copy(probsT[:, s.slot(2), 0:4, :], pp[:, 0:4, :]).then_inc(p_out[0].sem, 1)

            def lower(s):
                b = s.slot(2)
                until(v_, scored, s.n + 1)
                until(v_, stored, s.n - U + 1)
                own_.link(nc.vector.tensor_reduce(mx[:, b, :].rearrange("p (y x) -> p x y", y=2), sc[:, b, :, :, :], AX, ALU.max))
                if even:
                    own_.mark(nc.vector.tensor_scalar(outs[:, s.slot(U), QUAD:QUAD + 4], mx[:, b, :], SCALE, None, ALU.mult))
                    nc.vector.tensor_scalar(negm[:, b, :], mx[:, b, :], -SCALE, None, ALU.mult).then_inc(lowered.sem, 1)
                else:
                    u = s.slot(U)
                    own_.link(nc.vector.scalar_tensor_tensor(mx[:, b, :], mx[:, b, :], SCALE, sinks[:, 4 * u:4 * u + 4],
                                                             ALU.mult, ALU.max))
                    own_.mark(nc.vector.tensor_tensor(sink_e[:, u, :], sinks[:, 4 * u:4 * u + 4], mx[:, b, :], ALU.subtract))
                    nc.vector.tensor_scalar(negm[:, b, :], mx[:, b, :], -1.0, None, ALU.mult).then_inc(lowered.sem, 1)

            def out(s):
                b = s.slot(U)
                if even:
                    until(v_, summed, s.n + 1)
                    nc.vector.tensor_copy(outs[:, s.slot(U), 0:QUAD], op).then_inc(o_out.sem, 1)
                else:
                    until(v_, exped, s.n + 1)
                    own_.link(nc.vector.tensor_tensor(den[:, b, :], den[:, b, :], sink_e[:, b, :], ALU.add))
                    own_.link(nc.vector.reciprocal(rden[:, b, :], den[:, b, :]))
                    until(v_, summed, s.n + 1)
                    nc.vector.tensor_tensor(outs[:, s.slot(U), :].rearrange("p (h c) -> p h c", h=4),
                                            op.rearrange("p (h c) -> p h c", h=4),
                                            rden[:, b, :].unsqueeze(2).broadcast_to([P, 4, HD]), ALU.mult).then_inc(o_out.sem, 1)

            def step(s):
                if s.plus(1).within(N):
                    lower(s.plus(1))
                probs_out(s)
                if not isinstance(s.n, int) or s.n >= 1:
                    out(s.plus(-1))
            lower(Step(0, 0, U))
            looped(v_, N, U, U, step, own_, 2 if even else 5, head=1)
            out(Step(N // U - 1, U - 1, U))


def project_out(K, layer):
    nc, ps = K.nc, K.ps
    even = layer == 0
    NK = 6 if even else DK
    GW = QUAD + 8
    loads = 2 if even else 1
    with K.phase(f"out{layer}") as (sb, sem, block):
        ht = sb("ht", [P, 2, D])
        w = sb("w", [P, 2, NK, D], F32R)
        cat = sb("cat", [P, 2, NK * P])
        ot = sb("ot", [P, 2, 3, GW]) if even else None
        catT = sb("catT", [P, 2, 2, NK, P], F32R)
        h2 = sb("h2", [P, 2, D])
        hn = sb("hn", [P, 2, D])
        hnT = sb("hnT", [P, DK, P])
        junk = sb("junk", [P, D], BF16)
        gain = sb("gain", [P, D])
        wr = sb("wr", [P, DK, NL])
        br = sb("br", [P, NL])
        lg = sb("lg", [P, 2, NL])
        ss, rs = sb("ss", [P, 2]), sb("rs", [P, 2])
        power = sb("power", [P, 1])
        if even:
            m, dm, wt, wd, ds = (sb(n, [P, s, 4]) for n, s in (("m", 1), ("dm", 3), ("wt", 3), ("wd", 3), ("ds", 1)))
            part = sb("part", [P, 3, QUAD])
        x_in, h_in = [sem("x_in0"), sem("x_in1")], [sem("h_in0"), sem("h_in1")]
        par_in, own, pool_own, ready = sem("par_in"), sem("own"), sem("pool_own"), sem("ready")
        joined, diffed, weighed = Count(sem("joined")), Count(sem("diffed")), Count(sem("weighed"))
        w_high, w_low = sem("w_high"), sem("w_low")
        c_turned, c_high, c_low = Count(sem("c_turned")), Count(sem("c_high")), Count(sem("c_low"), 2)
        n_turned, n_out = Count(sem("n_turned")), Count(sem("n_out"))
        proj, added, sum_x, rms_x = Count(sem("proj")), Count(sem("added"), 2), Count(sem("sum_x"), 1), Count(sem("rms_x"))
        normed, routed, logged = Count(sem("normed")), Count(sem("routed")), Count(sem("logged"), 1)
        st, stored, st_lg, lg_stored = sem("st"), Count(sem("stored"), 2), sem("st_lg"), Count(sem("lg_stored"), 2)
        cp = ps[:, 0:NK * P]
        np_ = ps[:, 1024:2048]
        yp = ps[:, 2048:3072]
        rp = ps[:, 3072:3072 + NL]

        @block.sync
        def _(sp):
            sp.wait_ge(ready, 1)
            sp.dma_start(gain[:, :], K.x["norm_ffn"][layer:layer + 1].broadcast_to([P, D])).then_inc(par_in, 16)
            with nc.allow_non_contiguous_dma("router weights, 144 KB"):
                sp.dma_start(wr[:, :, 0:GROUPS], K.x["w_router_g"][layer].rearrange("(p k) g -> p k g", k=DK)).then_inc(par_in, 16)
                for g in range(GROUPS):
                    sp.dma_start(wr[:, :, GROUPS + g * EPG:GROUPS + (g + 1) * EPG],
                                 K.x["w_router_e"][layer, g].rearrange("(p k) e -> p k e", k=DK)).then_inc(par_in, 16)
            sp.dma_start(br[:, 0:GROUPS], K.x["b_router_g"][layer:layer + 1].broadcast_to([P, GROUPS])).then_inc(par_in, 16)
            sp.dma_start(br[:, GROUPS:NL], K.x["b_router_e"][layer:layer + 1].rearrange("a g e -> a (g e)").broadcast_to([P, NE])).then_inc(par_in, 16)

            def load_h(s):
                j, n = s.slot(2), s.n
                alone(sp, added, n - 1, K.tick_sp)
                src = K.x["x"].rearrange("a t c -> (a t) c") if even else K.h_d[0][0:T]
                sp.dma_start(ht[:, j, :], rows(src, n)).then_inc(h_in[j], 16)

            def load(s):
                j, n = s.slot(2), s.n
                if not isinstance(n, int) or n >= 2:
                    alone(sp, c_turned, n - 1, K.tick_sp)
                if even:
                    sp.dma_start(cat[:, j, 0:SGU], rows(K.a_d, n)).then_inc(x_in[j], 16)
                    sp.dma_start(ot[:, j, :, :].rearrange("p g c -> p (g c)"), rows(K.o_d, n)).then_inc(x_in[j], 16)
                else:
                    sp.dma_start(cat[:, j, :], rows(K.o1_d, n)).then_inc(x_in[j], 16)
            def step(s):
                n, j = s.n, s.slot(2)
                if s.plus(2).within(NT):
                    load(s.plus(2))
                alone(sp, added, n + 1, K.tick_sp)
                sp.dma_start(rows(K.h_d[layer][0:T], n), h2[:, j, :]).then_inc(st, 16)
                if s.plus(2).within(NT):
                    load_h(s.plus(2))
                alone(sp, normed, n + 1, K.tick_sp)
                sp.dma_start(rows(K.hn_d[layer], n), hn[:, j, :]).then_inc(st, 16)
                sp.wait_ge(st, n * 32 + 32)
                sp.sem_inc(stored.sem, 1)
                if not isinstance(n, int) or n >= 2:
                    store_lg(s.plus(-2))

            def store_lg(s):
                alone(sp, logged, s.n + 1, K.tick_sp)
                sp.dma_start(rows(K.lg_d[layer], s.n), lg[:, s.slot(2), :]).then_inc(st_lg, 16)
                sp.wait_ge(st_lg, s.n * 16 + 16)
                sp.sem_inc(lg_stored.sem, 1)
            for c in (stored, lg_stored):
                sp.sem_inc(c.sem, c.credit)
            s0 = Step(0, 0, 2)
            for s in (s0, s0.plus(1)):
                load(s)
                load_h(s)
            step(s0)
            for e in range(2):
                load_expert(K, sp, layer, e, e)
            step(s0.plus(1))
            with sp.Fori(1, NT // 2 - 1) as i:
                for j in range(2):
                    step(Step(i, j, 2))
            end = Step(NT // 2 - 1, 0, 2)
            step(end)
            step(end.plus(1))
            store_lg(end)
            store_lg(end.plus(1))

        @block.tensor
        def _(pe):

            def turn_cat(s):
                j = s.slot(2)
                if even:
                    until(pe, joined, s.n + 1)
                else:
                    pe.wait_ge(x_in[j], s.turn(2) * 16 + 16)
                until(pe, c_low, s.n)
                src = cat[:, j, :].rearrange("p (c k) -> p k c", k=NK)
                for k in range(NK):
                    last = nc.tensor.transpose(cp[:, k * P:(k + 1) * P], src[:, k, :], K.ident[:, :])
                last.then_inc(c_turned.sem, 1)

            def turn_hn(s):
                until(pe, normed, s.n + 1)
                src = hn[:, s.slot(2), :].rearrange("p (c k) -> p k c", k=DK)
                for k in range(DK):
                    last = nc.tensor.transpose(np_[:, k * P:(k + 1) * P], src[:, k, :], K.ident[:, :])
                last.then_inc(n_turned.sem, 1)

            def project(s):
                until(pe, c_high, s.n + 1)
                until(pe, added, s.n)
                for half in range(2):
                    for a, b in ((0, 0), (0, 1), (1, 0)):
                        if half == 0 and a == 1:
                            until(pe, c_low, s.n + 1)
                        for k in range(NK):
                            last = nc.tensor.matmul(yp[:, 512 * half:512 * (half + 1)], catT[:, s.slot(2), a, k, :],
                                                    w[:, b, k, 512 * half:512 * (half + 1)],
                                                    start=(a + b + k == 0), stop=(a == 1 and k == NK - 1))
                last.then_inc(proj.sem, 1)

            def router(s):
                until(pe, n_out, s.n + 1)
                until(pe, logged, s.n)
                for k in range(DK):
                    last = nc.tensor.matmul(rp, hnT[:, k, :], wr[:, k, :], start=(k == 0), stop=(k == DK - 1))
                last.then_inc(routed.sem, 1)

            def step(s):
                project(s)
                if s.plus(1).within(NT):
                    turn_cat(s.plus(1))
                if not isinstance(s.n, int) or s.n >= 2:
                    router(s.plus(-2))
                if not isinstance(s.n, int) or s.n >= 1:
                    turn_hn(s.plus(-1))
            s0 = Step(0, 0, 2)
            turn_cat(s0)
            pe.wait_ge(w_low, 2)
            pe.wait_ge(par_in, 16 * 8)
            step(s0)
            step(s0.plus(1))
            with pe.Fori(1, NT // 2 - 1) as i:
                for j in range(2):
                    step(Step(i, j, 2))
            end = Step(NT // 2 - 1, 0, 2)
            step(end)
            step(end.plus(1))
            router(end)
            turn_hn(end.plus(1))
            router(end.plus(1))

        @block.scalar
        def _(a):
            if even:
                def weights(s):
                    until(a, diffed, s.n + 1)
                    nc.scalar.activation(wt[:, :, :], dm[:, :, :], ACT.Exp).then_inc(weighed.sem, 1)
                weights(Step(0, 0, 2))
            a.wait_ge(K.weights_in[6 if even else 7], 16)
            for half in range(2):
                at = slice(512 * half, 512 * (half + 1))
                nc.scalar.activation(w[:, 0, :, at], K.w_out[:, :, at], ACT.Copy).then_inc(w_high, 1)

            def cat_out(s):
                until(a, c_turned, s.n + 1)
                if not isinstance(s.n, int) or s.n >= 2:
                    until(a, proj, s.n - 1)
                nc.scalar.activation(catT[:, s.slot(2), 0, :, :], cp.rearrange("p (k c) -> p k c", k=NK), ACT.Copy).then_inc(c_high.sem, 1)
            a.sem_inc(sum_x.sem, sum_x.credit)

            def step(s):
                if s.plus(1).within(NT):
                    if even:
                        weights(s.plus(1))
                    cat_out(s.plus(1))
                until(a, added, s.n + 1)
                until(a, sum_x, s.n)
                nc.scalar.activation(junk[:, :], h2[:, s.slot(2), :], ACT.Square, accum_out=ss[:, s.slot(2):s.slot(2) + 1]).then_inc(sum_x.sem, 1)
            cat_out(Step(0, 0, 2))
            looped(a, NT, 2, 2, step, head=1)

        @block.gpsimd
        def _(g):
            own_ = Chain(g, pool_own)
            own_.link(g.memset(power[:, :], -0.5))

            def step(s):
                j = s.slot(2)
                alone(g, sum_x, s.n + 1, K.tick)
                own_.link(g.tensor_scalar(rs[:, j:j + 1], ss[:, j:j + 1], 1.0 / D, EPS, ALU.mult, ALU.add))
                g.tensor_tensor(rs[:, j:j + 1], rs[:, j:j + 1], power[:, 0:1], ALU.pow).then_inc(rms_x.sem, 1)
            looped(g, NT, 2, 0, step, own_, 1)

        @block.vector
        def _(v_):
            own_ = Chain(v_, own)
            for c in (c_low, added, logged):
                v_.sem_inc(c.sem, c.credit)
            v_.sem_inc(ready, 1)

            def join(s):
                j = s.slot(2)
                v_.wait_ge(x_in[j], s.turn(2) * (16 * loads) + 16 * loads)
                if not even:
                    return
                mm, dd = ot[:, j, :, QUAD:QUAD + 4], ot[:, j, :, QUAD + 4:QUAD + 8]
                own_.link(nc.vector.tensor_tensor(m[:, 0, :], mm[:, 0, :], mm[:, 1, :], ALU.max))
                own_.link(nc.vector.tensor_tensor(m[:, 0, :], m[:, 0, :], mm[:, 2, :], ALU.max))
                nc.vector.tensor_tensor(dm[:, :, :], mm, m[:, :, :].broadcast_to([P, 3, 4]), ALU.subtract).then_inc(diffed.sem, 1)
                until(v_, weighed, s.n + 1)
                own_.link(nc.vector.tensor_tensor(wd[:, :, :], wt[:, :, :], dd, ALU.mult))
                own_.link(nc.vector.tensor_tensor(ds[:, 0, :], wd[:, 0, :], wd[:, 1, :], ALU.add))
                own_.link(nc.vector.tensor_tensor(ds[:, 0, :], ds[:, 0, :], wd[:, 2, :], ALU.add))
                own_.link(nc.vector.reciprocal(ds[:, 0, :], ds[:, 0, :]))
                own_.link(nc.vector.tensor_tensor(wd[:, :, :], wt[:, :, :], ds[:, :, :].broadcast_to([P, 3, 4]), ALU.mult))
                for g in range(3):
                    own_.mark(nc.vector.tensor_tensor(part[:, g, :].rearrange("p (h c) -> p h c", h=4),
                                                      ot[:, j, g, 0:QUAD].rearrange("p (h c) -> p h c", h=4),
                                                      wd[:, g, :].unsqueeze(2).broadcast_to([P, 4, HD]), ALU.mult))
                own_.meet()
                own_.link(nc.vector.tensor_tensor(part[:, 0, :], part[:, 0, :], part[:, 1, :], ALU.add))
                nc.vector.tensor_tensor(cat[:, j, SGU:SGU + QUAD], part[:, 0, :], part[:, 2, :], ALU.add).then_inc(joined.sem, 1)

            def cat_out(s):
                j = s.slot(2)
                until(v_, c_high, s.n + 1)
                nc.vector.tensor_tensor(catT[:, j, 1, :, :], cp.rearrange("p (k c) -> p k c", k=NK),
                                        catT[:, j, 0, :, :].bitcast(F32), ALU.subtract).then_inc(c_low.sem, 1)

            def hn_out(s):
                until(v_, n_turned, s.n + 1)
                nc.vector.tensor_copy(hnT[:, :, :], np_.rearrange("p (k c) -> p k c", k=DK)).then_inc(n_out.sem, 1)

            def add(s):
                j = s.slot(2)
                v_.wait_ge(h_in[j], s.turn(2) * 16 + 16)
                until(v_, proj, s.n + 1)
                until(v_, stored, s.n - 1)
                nc.vector.tensor_tensor(h2[:, j, :], yp, ht[:, j, :], ALU.add).then_inc(added.sem, 1)

            def norm(s):
                j = s.slot(2)
                until(v_, rms_x, s.n + 1)
                nc.vector.scalar_tensor_tensor(hn[:, j, :], h2[:, j, :], rs[:, j:j + 1], gain[:, :], ALU.mult, ALU.mult).then_inc(normed.sem, 1)

            def log(s):
                j = s.slot(2)
                until(v_, routed, s.n + 1)
                until(v_, lg_stored, s.n - 1)
                nc.vector.tensor_tensor(lg[:, j, :], rp, br[:, :], ALU.add).then_inc(logged.sem, 1)

            def step(s):
                if not isinstance(s.n, int) or s.n >= 1:
                    norm(s.plus(-1))
                if s.plus(1).within(NT):
                    join(s.plus(1))
                add(s)
                if s.plus(1).within(NT):
                    cat_out(s.plus(1))
                if not isinstance(s.n, int) or s.n >= 2:
                    log(s.plus(-2))
                if not isinstance(s.n, int) or s.n >= 1:
                    hn_out(s.plus(-1))
            s0 = Step(0, 0, 2)
            join(s0)
            for half in range(2):
                at = slice(512 * half, 512 * (half + 1))
                v_.wait_ge(w_high, half + 1)
                nc.vector.tensor_tensor(w[:, 1, :, at], K.w_out[:, :, at], w[:, 0, :, at].bitcast(F32), ALU.subtract).then_inc(w_low, 1)
            cat_out(s0)
            v_.wait_ge(par_in, 16 * 8)
            step(s0)
            step(s0.plus(1))
            per, start = (11 if even else 0), own_.n
            with v_.Fori(1, NT // 2 - 1) as i:
                own_.base, own_.n = (i - 1) * (2 * per) + start, 0
                for j in range(2):
                    step(Step(i, j, 2))
                assert own_.n == 2 * per, own_.n / 2
            own_.base, own_.n = start + (NT // 2 - 2) * 2 * per, 0
            end = Step(NT // 2 - 1, 0, 2)
            step(end)
            step(end.plus(1))
            log(end)
            norm(end.plus(1))
            hn_out(end.plus(1))
            log(end.plus(1))


def load_expert(K, sp, layer, e, slot, until_free=lambda n: None):
    nc = K.nc
    for n, name in enumerate(("w_gate", "w_up")):
        until_free(n)
        src = K.x[name][layer].rearrange("e (p k) f -> e p (k f)", k=DK)
        src = src[e] if isinstance(e, int) else src[bass.ds(e, 1)].rearrange("a p f -> (a p) f")
        dst = K.expert_w[:, slot, n * DK * FF:(n + 1) * DK * FF]
        sp.dma_start(dst, src).then_inc(K.expert_in[layer][slot], 16)
    until_free(2)
    src = K.x["w_down"][layer].rearrange("e (p k) n -> e p (k n)", k=2)
    src = src[e] if isinstance(e, int) else src[bass.ds(e, 1)].rearrange("a p n -> (a p) n")
    sp.dma_start(K.expert_w[:, slot, DK * 2 * FF:], src).then_inc(K.expert_in[layer][slot], 16)


def route(K, layer):
    nc, ps = K.nc, K.ps
    with K.phase(f"route{layer}") as (sb, sem, block):
        lg = sb("lg", [P, NT, NL])
        iota4, iota32 = sb("iota4", [P, GROUPS]), sb("iota32", [P, NE])
        iota_i = sb("iota_i", [P, NE], I32)
        gm, gi, gs = sb("gm", [P, NT]), sb("gi", [P, NT]), sb("gs", [P, NT])
        gx, gone = sb("gx", [P, NT, GROUPS]), sb("gone", [P, NT, GROUPS])
        le, cand = sb("le", [P, NT, NE]), sb("cand", [P, NT, NE])
        one = sb("one", [P, 2, NT, NE])
        both = sb("both", [P, NT, NE], BF16)
        best = sb("best", [P, 2, NT])
        rank, base = sb("rank", [P, NT, NE]), sb("base", [P, NT, NE])
        e2, gate = sb("e2", [P, NT]), sb("gate", [P, 2, NT])
        count, blocks, ends, zero = (sb(n, [P, NE]) for n in ("count", "blocks", "ends", "zero"))
        count_i = sb("count_i", [P, NE], I32)
        place, place_i, low_i, high_i = sb("place", [P, 2, NT]), *(sb(n, [P, 2, NT], I32) for n in ("place_i", "low_i", "high_i"))
        low, high = sb("low", [P, 2, NT]), sb("high", [P, 2, NT])
        token = sb("token", [P, NT], I32)
        token_f = sb("token_f", [P, NT])
        iota_p, iota_row = sb("iota_p", [P, P], I32), sb("iota_row", [P, P])
        spare_i, spare = sb("spare_i", [P, 1], I32), sb("spare", [P, 1])
        at_row = K.out_w[:, 0:2 * NT * P].rearrange("p (n c) -> p n c", c=P)
        at_block = sb("at_block", [P, 2 * NT, 3, NBMAX])
        found = sb("found", [P, 3, NBMAX])
        in_, own, pool_own, exp_in, exp_out = (sem(n) for n in ("in", "own", "pool_own", "exp_in", "exp_out"))
        made, both_done, counted, placed, gathered = (sem(n) for n in
            ("made", "both_done", "counted", "placed", "gathered"))
        table = ps[:, 1024:1024 + 3 * NBMAX].rearrange("p (f b) -> p f b", f=3)
        wide4, wide32 = [P, NT, GROUPS], [P, NT, NE]
        pre = ps[:, 0:NT * NE].rearrange("p (n e) -> p n e", n=NT)
        tot = ps[:, 512:512 + NT * NE].rearrange("p (n e) -> p n e", n=NT)

        @block.sync
        def _(sp):
            sp.dma_start(lg[:, :, :], K.lg_d[layer].rearrange("(n p) c -> p n c", p=P)).then_inc(in_, 16)

        @block.gpsimd
        def _(g):
            g.iota(iota_i[:, :], pattern=[[1, NE]], base=0, channel_multiplier=0).then_inc(made, 1)
            g.iota(token[:, :], pattern=[[P, NT]], base=0, channel_multiplier=1).then_inc(made, 1)
            g.iota(iota_p[:, :], pattern=[[1, P]], base=0, channel_multiplier=0).then_inc(made, 1)
            g.iota(spare_i[:, :], pattern=[[0, 1]], base=T, channel_multiplier=1).then_inc(made, 1)

        @block.scalar
        def _(a):
            a.wait_ge(exp_in, 1)
            nc.scalar.activation(gx[:, :, :], gx[:, :, :], ACT.Exp).then_inc(exp_out, 1)
            a.wait_ge(exp_in, 2)
            nc.scalar.activation(e2[:, :], e2[:, :], ACT.Exp).then_inc(exp_out, 1)

        @block.tensor
        def _(pe):
            pe.wait_ge(both_done, 1)
            flat = both[:, :, :].rearrange("p n e -> p (n e)")
            nc.tensor.matmul(ps[:, 0:NT * NE], K.before[:, :], flat, start=True, stop=True)
            nc.tensor.matmul(ps[:, 512:512 + NT * NE], K.onesb[:, :], flat, start=True, stop=True).then_inc(counted, 1)
            pe.wait_ge(placed, 1)
            for n in range(2 * NT):
                last = nc.tensor.matmul(table, at_row[:, n, :], at_block[:, n, :, :], start=(n == 0), stop=(n == 2 * NT - 1))
            last.then_inc(gathered, 1)

        @block.vector
        def _(v):
            V = nc.vector
            own_ = Chain(v, own)
            do = own_.link
            v.wait_ge(made, 4)
            do(V.tensor_copy(iota32[:, :], iota_i[:, :]))
            do(V.tensor_copy(iota4[:, :], iota_i[:, 0:GROUPS]))
            do(V.tensor_copy(token_f[:, :], token[:, :]))
            do(V.memset(zero[:, :], 0.0))
            do(V.tensor_copy(iota_row[:, :], iota_p[:, :]))
            do(V.tensor_copy(spare[:, :], spare_i[:, :]))
            v.wait_ge(in_, 16)
            lgg = lg[:, :, 0:GROUPS]
            i4 = iota4[:, :].unsqueeze(1).broadcast_to(wide4)
            i32 = iota32[:, :].unsqueeze(1).broadcast_to(wide32)

            def bc(t, wide):
                return t.unsqueeze(2).broadcast_to(wide)

            do(V.tensor_reduce(gm[:, :], lgg, AX, ALU.max))
            do(V.tensor_tensor(gx[:, :, :], lgg, bc(gm[:, :], wide4), ALU.is_lt))
            do(V.scalar_tensor_tensor(gx[:, :, :], gx[:, :, :], BIG, i4, ALU.mult, ALU.add))
            do(V.tensor_reduce(gi[:, :], gx[:, :, :], AX, ALU.min))
            do(V.tensor_tensor(gone[:, :, :], i4, bc(gi[:, :], wide4), ALU.is_equal))
            V.tensor_tensor(gx[:, :, :], lgg, bc(gm[:, :], wide4), ALU.subtract).then_inc(exp_in, 1)
            leg = le[:, :, :].rearrange("p n (g e) -> p (n g) e", g=GROUPS)
            go = gone[:, :, :].rearrange("p n g -> p (n g)").unsqueeze(2).broadcast_to([P, NT * GROUPS, EPG])
            do(V.tensor_copy(le[:, :, :], lg[:, :, GROUPS:NL]))
            do(V.tensor_tensor(leg, leg, go, ALU.mult))
            do(V.tensor_scalar(gone[:, :, :], gone[:, :, :], -NEG, NEG, ALU.mult, ALU.add))
            do(V.tensor_tensor(leg, leg, go, ALU.add))
            for k in range(2):
                do(V.tensor_reduce(best[:, k, :], le[:, :, :], AX, ALU.max))
                do(V.tensor_tensor(cand[:, :, :], le[:, :, :], bc(best[:, k, :], wide32), ALU.is_lt))
                do(V.scalar_tensor_tensor(cand[:, :, :], cand[:, :, :], BIG, i32, ALU.mult, ALU.add))
                do(V.tensor_reduce(gi[:, :], cand[:, :, :], AX, ALU.min))
                do(V.tensor_tensor(one[:, k, :, :], i32, bc(gi[:, :], wide32), ALU.is_equal))
                if k == 0:
                    do(V.scalar_tensor_tensor(le[:, :, :], one[:, 0, :, :], 2 * NEG, le[:, :, :], ALU.mult, ALU.add))
            V.tensor_tensor(both[:, :, :], one[:, 0, :, :], one[:, 1, :, :], ALU.add).then_inc(both_done, 1)
            V.tensor_tensor(e2[:, :], best[:, 1, :], best[:, 0, :], ALU.subtract).then_inc(exp_in, 1)
            v.wait_ge(exp_out, 2)
            do(V.tensor_reduce(gs[:, :], gx[:, :, :], AX, ALU.add))
            do(V.tensor_scalar(best[:, 0, :], e2[:, :], 1.0, None, ALU.add))
            do(V.tensor_tensor(gs[:, :], gs[:, :], best[:, 0, :], ALU.mult))
            do(V.reciprocal(gate[:, 0, :], gs[:, :]))
            do(V.tensor_tensor(gate[:, 1, :], gate[:, 0, :], e2[:, :], ALU.mult))
            v.wait_ge(counted, 1)
            do(V.memset(base[:, 0, :], 0.0))
            for n in range(1, NT):
                do(V.tensor_tensor(base[:, n, :], base[:, n - 1, :], tot[:, n - 1, :], ALU.add))
            do(V.tensor_tensor(count[:, :], base[:, NT - 1, :], tot[:, NT - 1, :], ALU.add))
            do(V.tensor_tensor(rank[:, :, :], base[:, :, :], pre, ALU.add))
            do(V.tensor_scalar(count_i[:, :], count[:, :], float(P - 1), None, ALU.add))
            do(V.tensor_scalar(count_i[:, :], count_i[:, :], 7, None, ALU.arith_shift_right))
            do(V.tensor_scalar(blocks[:, :], count_i[:, :], 1.0, None, ALU.max))
            do(V.tensor_tensor_scan(ends[:, :], blocks[:, :], zero[:, :], 0.0, ALU.add, ALU.add))
            do(V.memset(K.ends_i[:, 0:1], 0))
            do(V.tensor_copy(K.ends_i[:, 1:NE + 1], ends[0:1, :]))
            do(V.tensor_tensor(ends[:, :], ends[:, :], blocks[:, :], ALU.subtract))
            do(V.scalar_tensor_tensor(rank[:, :, :], ends[:, :].unsqueeze(1).broadcast_to(wide32), float(P), rank[:, :, :],
                                      ALU.mult, ALU.add))
            for k in range(2):
                do(V.tensor_tensor(one[:, k, :, :], one[:, k, :, :], rank[:, :, :], ALU.mult))
                do(V.tensor_reduce(place[:, k, :], one[:, k, :, :], AX, ALU.add))
            do(V.tensor_copy(place_i[:, :, :], place[:, :, :]))
            do(V.tensor_scalar(low_i[:, :, :], place_i[:, :, :], P - 1, None, ALU.bitwise_and))
            do(V.tensor_scalar(high_i[:, :, :], place_i[:, :, :], 7, None, ALU.arith_shift_right))
            do(V.tensor_copy(low[:, :, :], low_i[:, :, :]))
            do(V.tensor_copy(high[:, :, :], high_i[:, :, :]))
            lows, highs, gates = (t[:, :, :].rearrange("p k n -> p (k n)") for t in (low, high, gate))
            rows_, blocks_ = [P, 2 * NT, P], [P, 2 * NT, NBMAX]
            own_.mark(V.tensor_tensor(at_row[:, :, :], iota_row[:, :].unsqueeze(1).broadcast_to(rows_),
                                      lows.unsqueeze(2).broadcast_to(rows_), ALU.is_equal))
            do(V.tensor_tensor(at_block[:, :, 0, :], iota_row[:, 0:NBMAX].unsqueeze(1).broadcast_to(blocks_),
                               highs.unsqueeze(2).broadcast_to(blocks_), ALU.is_equal))
            for k in range(2):
                at = slice(k * NT, (k + 1) * NT)
                own_.mark(V.tensor_tensor(at_block[:, at, 1, :], at_block[:, at, 0, :],
                                          token_f[:, :].unsqueeze(2).broadcast_to([P, NT, NBMAX]), ALU.mult))
            do(V.tensor_tensor(at_block[:, :, 2, :], at_block[:, :, 0, :], gates.unsqueeze(2).broadcast_to(blocks_), ALU.mult))
            v.sem_inc(placed, 1)
            v.wait_ge(gathered, 1)
            do(V.tensor_copy(found[:, :, :], table))
            own_.mark(V.tensor_copy(K.who[:, :], found[:, 1, :]))
            own_.mark(V.tensor_copy(K.gates[:, :], found[:, 2, :]))
            do(V.tensor_scalar(found[:, 0, :], found[:, 0, :], -1.0, 1.0, ALU.mult, ALU.add))
            do(V.scalar_tensor_tensor(K.where[:, :], found[:, 0, :], spare[:, 0:1], found[:, 1, :], ALU.mult, ALU.add))


def experts(K, layer):
    nc, ps = K.nc, K.ps
    GU, EW = DK * 2 * FF, DK * 2 * FF + 2 * D
    PIECE = 1024
    GU_PIECES, PIECES = GU // PIECE, EW // PIECE
    with K.phase(f"moe{layer}") as (sb, sem, block):
        xg = sb("xg", [P, D])
        xT = sb("xT", [P, 2, DK, P], F32R)
        silu, hid = sb("silu", [P, FF]), sb("hid", [P, FF])
        hidT = sb("hidT", [P, 2, 2, P], F32R)
        y = sb("y", [P, D])
        who, where = sb("who", [P, 1], I32), sb("where", [P, 1], I32)
        gate = sb("gate", [P, 1])
        parts = sb("parts", [P, 2, 2, EW], F32R)
        gathered_s, scattered_s = sem("gathered"), sem("scattered")
        who_set, where_set = Count(sem("who_set")), Count(sem("where_set"))
        x_turned, x_high, x_low = Count(sem("x_turned")), Count(sem("x_high")), Count(sem("x_low"))
        w_high, w_low = Count(sem("w_high")), Count(sem("w_low"))
        up, act_done, hid_done = Count(sem("up")), Count(sem("act_done")), Count(sem("hid_done"), 1)
        h_turned, h_high, h_low, down = Count(sem("h_turned")), Count(sem("h_high")), Count(sem("h_low")), Count(sem("down"))
        y_out, gated = Count(sem("y_out"), 1), Count(sem("gated"))
        gup = ps[:, 0:2 * FF]
        xp = ps[:, 512:512 + D]
        hp = ps[:, 1536:1536 + 2 * P]
        yp = ps[:, 2048:2048 + D]
        lim = dict(min_val=1, max_val=64)

        def end_of(eng, at):
            src = K.ends_i[0:1, at:at + 1] if isinstance(at, int) else K.ends_i[0:1, bass.ds(at, 1)]
            return eng.value_load(src, **lim)

        def in_turn(eng, first_block, block):
            def pair(i, is_first, is_last):
                for j in range(2):
                    e = i * 2 + j
                    m0 = 0 if is_first and j == 0 else end_of(eng, e)
                    first_block(i, j, m0, not (is_first and j == 0), not (is_last and j == 1))
                    end = end_of(eng, e + 1)
                    with eng.If(end > m0 + 1):
                        with eng.Fori(m0 + 1, end) as m:
                            block(m, j)
            pair(0, True, False)
            with eng.Fori(1, NE // 2 - 1) as i:
                pair(i, False, False)
            pair(NE // 2 - 1, False, True)

        @block.sync
        def _(sp):
            def load(i, j):
                load_expert(K, sp, layer, i * 2 + j, j, lambda n: alone(
                    sp, w_low, i * (2 * PIECES) + ((j - 2) * PIECES + (n + 1) * PIECES // 3), K.tick_sp))
            with sp.Fori(1, NE // 2) as i:
                for j in range(2):
                    load(i, j)
            if layer == 0:
                sp.wait_ge(w_low.sem, NE * PIECES)
                sp.dma_start(K.w_in_odd, K.x["w_in_odd"].rearrange("a (p k) n -> p (a k) n", k=DK)).then_inc(K.weights_in[5], 16)

        @block.gpsimd
        def _(g):
            def gather(m):
                nc.gpsimd.tensor_copy(who[:, :], K.who[:, m:m + 1] if isinstance(m, int) else K.who[:, bass.ds(m, 1)]).then_inc(who_set.sem, 1)
                alone(g, who_set, m + 1, K.tick)
                nc.gpsimd.indirect_dma_start(xg[:, :], None, K.hn_d[layer],
                                             bass.IndirectOffsetOnAxis(ap=who[:, :], axis=0)).then_inc(gathered_s, 16)

            def set_gate(m):
                nc.gpsimd.tensor_copy(gate[:, :], K.gates[:, bass.ds(m, 1)]).then_inc(gated.sem, 1)

            def scatter(m):
                g.wait_ge(scattered_s, m * 16 + 16)
                g.sem_inc(K.tick, 1)
                nc.gpsimd.tensor_copy(where[:, :], K.where[:, bass.ds(m, 1)]).then_inc(where_set.sem, 1)
                alone(g, where_set, m + 1, K.tick)
                alone(g, y_out, m + 1, K.tick)
                nc.gpsimd.indirect_dma_start(K.h_d[layer], bass.IndirectOffsetOnAxis(ap=where[:, :], axis=0), y[:, :], None,
                                             compute_op=ALU.add).then_inc(scattered_s, 16)
            gather(0)
            g.dma_start(where[:, :], K.where[:, 0:1]).then_inc(scattered_s, 16)
            g.wait_ge(gathered_s, 16)
            until(g, x_turned, 1)
            gather(1)
            until(g, x_turned, 2)
            gather(2)
            total = end_of(g, NE)
            with g.Fori(1, total) as m:
                set_gate(m - 1)
                alone(g, x_turned, m + 2, K.tick)
                gather(m + 2)
                scatter(m - 1)
            set_gate(total - 1)
            scatter(total - 1)
            g.wait_ge(gathered_s, total * 16 + 32)
            g.sem_inc(K.tick, 1)
            g.wait_ge(scattered_s, total * 16 + 16)
            g.sem_inc(K.tick, 1)

        @block.tensor
        def _(pe):
            def product(out, left, right, K_):
                for n, (a, b) in enumerate(((0, 0), (0, 1), (1, 0))):
                    for k in range(K_):
                        last = nc.tensor.matmul(out, left[:, a, k, :], right(b, k), start=(n == 0 and k == 0),
                                                stop=(n == 2 and k == K_ - 1))
                return last

            def turn_x(m):
                pe.wait_ge(gathered_s, m * 16 + 16)
                src = xg[:, :].rearrange("p (c k) -> p k c", k=DK)
                for k in range(DK):
                    last = nc.tensor.transpose(xp[:, k * P:(k + 1) * P], src[:, k, :], K.ident[:, :])
                last.then_inc(x_turned.sem, 1)

            def raise_(m, j):
                wgu = parts[:, j, :, 0:GU].rearrange("p h (s k f) -> p h k s f", s=2, k=DK)
                until(pe, x_low, m + 1)
                until(pe, hid_done, m)
                product(gup, xT, lambda h, k: wgu[:, h, k, :, :], DK).then_inc(up.sem, 1)

            def turn_hid(m):
                until(pe, hid_done, m + 1)
                src = hid[:, :].rearrange("p (c k) -> p k c", k=2)
                for k in range(2):
                    last = nc.tensor.transpose(hp[:, k * P:(k + 1) * P], src[:, k, :], K.ident[:, :])
                last.then_inc(h_turned.sem, 1)

            def lower(m, j):
                wd = parts[:, j, :, GU:EW].rearrange("p h (k n) -> p h k n", k=2)
                until(pe, h_low, m + 1)
                until(pe, y_out, m)
                for half in range(2):
                    last = product(yp[:, 512 * half:512 * (half + 1)], hidT,
                                   lambda h, k: wd[:, h, k, 512 * half:512 * (half + 1)], 2)
                last.then_inc(down.sem, 1)

            def first_block(i, j, m, behind, ahead):
                if behind:
                    turn_hid(m - 1)
                pe.wait_ge(w_low.sem, i * (2 * PIECES) + j * PIECES + GU_PIECES)
                raise_(m, j)
                turn_x(m + 1)
                if behind:
                    lower(m - 1, 1 - j)
                pe.wait_ge(w_low.sem, i * (2 * PIECES) + (j + 1) * PIECES)
                pe.sem_inc(K.tick_pe, 1)

            def block_(m, j):
                turn_hid(m - 1)
                raise_(m, j)
                turn_x(m + 1)
                lower(m - 1, j)
            turn_x(0)
            in_turn(pe, first_block, block_)
            total = end_of(pe, NE)
            turn_hid(total - 1)
            lower(total - 1, 1)

        @block.scalar
        def _(a):
            a.sem_inc(y_out.sem, y_out.credit)

            def split(i, j, pieces):
                for n in pieces:
                    at = slice(n * PIECE, (n + 1) * PIECE)
                    nc.scalar.activation(parts[:, j, 0, at], K.expert_w[:, j, at], ACT.Copy).then_inc(w_high.sem, 1)

            def x_out(m):
                until(a, x_turned, m + 1)
                nc.scalar.activation(xT[:, 0, :, :], xp.rearrange("p (k c) -> p k c", k=DK), ACT.Copy).then_inc(x_high.sem, 1)

            def act(m):
                until(a, up, m + 1)
                nc.scalar.activation(silu[:, :], gup[:, 0:FF], ACT.Silu).then_inc(act_done.sem, 1)

            def y_scaled(m):
                until(a, down, m + 1)
                until(a, gated, m + 1)
                a.wait_ge(scattered_s, m * 16 + 16)
                nc.scalar.activation(y[:, :], yp, ACT.Copy, scale=gate[:, 0:1]).then_inc(y_out.sem, 1)

            def first_block(i, j, m, behind, ahead):
                ni, nj = i + j, 1 - j
                if ahead:
                    a.wait_ge(K.expert_in[layer][nj], ni * 48 + 48)
                    if behind:
                        until(a, up, m)
                    split(ni, nj, range(GU_PIECES))
                act(m)
                x_out(m + 1)
                if behind:
                    y_scaled(m - 1)
                if ahead:
                    split(ni, nj, range(GU_PIECES, PIECES))

            def block_(m, j):
                act(m)
                x_out(m + 1)
                y_scaled(m - 1)
            a.wait_ge(K.expert_in[layer][0], 48)
            split(0, 0, range(PIECES))
            x_out(0)
            in_turn(a, first_block, block_)
            y_scaled(end_of(a, NE) - 1)

        @block.vector
        def _(v):
            v.sem_inc(hid_done.sem, hid_done.credit)

            def split(i, j, pieces):
                for n in pieces:
                    at = slice(n * PIECE, (n + 1) * PIECE)
                    v.wait_ge(w_high.sem, i * (2 * PIECES) + (j * PIECES + n + 1))
                    nc.vector.tensor_tensor(parts[:, j, 1, at], K.expert_w[:, j, at], parts[:, j, 0, at].bitcast(F32),
                                            ALU.subtract).then_inc(w_low.sem, 1)

            def x_out(m):
                until(v, x_high, m + 1)
                nc.vector.tensor_tensor(xT[:, 1, :, :], xp.rearrange("p (k c) -> p k c", k=DK), xT[:, 0, :, :].bitcast(F32),
                                        ALU.subtract).then_inc(x_low.sem, 1)

            def hid_out(m):
                until(v, h_turned, m + 1)
                hpk = hp.rearrange("p (k c) -> p k c", k=2)
                nc.vector.tensor_copy(hidT[:, 0, :, :], hpk).then_inc(h_high.sem, 1)
                until(v, h_high, m + 1)
                nc.vector.tensor_tensor(hidT[:, 1, :, :], hpk, hidT[:, 0, :, :].bitcast(F32), ALU.subtract).then_inc(h_low.sem, 1)

            def hidden(m):
                until(v, act_done, m + 1)
                nc.vector.tensor_tensor(hid[:, :], silu[:, :], gup[:, FF:2 * FF], ALU.mult).then_inc(hid_done.sem, 1)

            def first_block(i, j, m, behind, ahead):
                ni, nj = i + j, 1 - j
                if ahead:
                    split(ni, nj, range(GU_PIECES // 2))
                if behind:
                    hid_out(m - 1)
                if ahead:
                    split(ni, nj, range(GU_PIECES // 2, GU_PIECES))
                hidden(m)
                x_out(m + 1)
                if ahead:
                    split(ni, nj, range(GU_PIECES, PIECES))

            def block_(m, j):
                hid_out(m - 1)
                hidden(m)
                x_out(m + 1)
            split(0, 0, range(PIECES))
            x_out(0)
            in_turn(v, first_block, block_)
            hid_out(end_of(v, NE) - 1)


NAMES = ["x", "positions", "norm_mix", "norm_ffn", "w_in_even", "w_out_even", "sgu_norm", "sgu_w", "sgu_b",
         "qn_dil", "kn_dil", "w_in_odd", "w_out_odd", "qn_swa", "kn_swa", "sinks", "w_router_g", "b_router_g",
         "w_router_e", "b_router_e", "w_gate", "w_up", "w_down"]


def kernel(**inputs):
    import concourse.bacc as bacc
    from concourse.bass_utils import run_bass_kernel_spmd

    nc = bacc.Bacc("TRN2", target_bir_lowering=False, num_devices=1)
    arrays, ins = {}, {}
    for name in NAMES:
        a = np.ascontiguousarray(inputs[name])
        arrays[f"in_{name}"] = a
        ins[name] = nc.dram_tensor(f"in_{name}", a.shape, mybir.dt.from_np(a.dtype), kind="ExternalInput").ap()
    out = nc.dram_tensor("out", (T + P, D), F32, kind="ExternalOutput").ap()
    Kernel(nc, ins, out).build()
    r = run_bass_kernel_spmd(nc, [arrays], core_ids=[0])
    return r.results[0]["out"][0:T].reshape(1, T, D)
```
